# Optimizing a Trainium2 kernel written in Bass

```python
import math
import jax, jax.numpy as jnp
from jax import lax
import numpy as np

D_MODEL = 1024
BATCH = 1
SEQ = 256
DEPTH = 1
DEC_BATCH = 8
DEC_SEQ = 8
PAST_LEN = 2048
PAGE_SIZE = 128

HG_HEADS = 8
HG_DK = 128
HG_DV = 128
HG_KW = HG_HEADS * HG_DK
HG_VW = HG_HEADS * HG_DV
HG_CHUNK = 64
HG_SCALE = HG_DK ** -0.5
S5_WIDTH = 512
S5_GROUP = 16
S5_GROUPS = S5_WIDTH // S5_GROUP
S5_STATE = 64
S5_DT_MIN = 0.001
S5_DT_MAX = 0.1
MOE_GROUPS = 4
MOE_EXPERTS_PER_GROUP = 8
N_EXPERTS = MOE_GROUPS * MOE_EXPERTS_PER_GROUP
MOE_TOP_K = 2
D_EXPERT = 512
RMS_EPS = 1e-6
IN_WIDTH = 2 * HG_KW + 2 * HG_VW + S5_WIDTH + 2 * D_MODEL
IN_SPLITS = (HG_KW, 2 * HG_KW, 2 * HG_KW + HG_VW, 2 * HG_KW + 2 * HG_VW,
             2 * HG_KW + 2 * HG_VW + S5_WIDTH, 2 * HG_KW + 2 * HG_VW + S5_WIDTH + D_MODEL)

kernel_name = "hgrn2_s5_hmoe_hybrid_step"

def rmsnorm(x, g):
    xf = x.astype(jnp.float32)
    return xf * lax.rsqrt(jnp.mean(xf * xf, axis=-1, keepdims=True) + RMS_EPS) * g.astype(jnp.float32)

def hgrn2_recurrence(q, k, v, log_f, s0):
    B, L, H, DK = q.shape
    DV = v.shape[-1]
    c = L if L <= HG_CHUNK else math.gcd(L, HG_CHUNK)
    n = L // c

    def to_chunks(t):
        return t.reshape(B, n, c, H, t.shape[-1]).transpose(1, 0, 3, 2, 4)

    qc, kc, vc, gc = to_chunks(q), to_chunks(k), to_chunks(v), to_chunks(log_f)
    causal = jnp.tril(jnp.ones((c, c), dtype=bool))

    def step(s, inp):
        qb, kb, vb, gb = inp
        b = jnp.cumsum(gb, axis=2)
        b_last = b[:, :, -1:, :]
        q_dec = qb * jnp.exp(b)
        k_dec = kb * jnp.exp(-b)
        scores = jnp.where(causal, jnp.einsum('bhtk,bhsk->bhts', q_dec, k_dec), 0.0)
        o = jnp.einsum('bhtk,bhkv->bhtv', q_dec, s) + jnp.einsum('bhts,bhsv->bhtv', scores, vb)
        s_new = (jnp.exp(b_last[:, :, 0, :])[..., None] * s
                 + jnp.einsum('bhsk,bhsv->bhkv', kb * jnp.exp(b_last - b), vb))
        return s_new, o

    s_final, o = lax.scan(step, s0, (qc, kc, vc, gc))
    o = o.transpose(1, 0, 3, 2, 4).reshape(B, L, H, DV)
    return o, s_final

def s5_branch(u, h0_re, h0_im, lam_re, lam_im, log_dt, b_re, b_im, c_re, c_im, d_skip):
    lam_re = lam_re.astype(jnp.float32)
    lam_im = lam_im.astype(jnp.float32)
    dt = jnp.exp(log_dt.astype(jnp.float32))[:, None]
    mag = jnp.exp(lam_re * dt)
    ab_re = mag * jnp.cos(lam_im * dt)
    ab_im = mag * jnp.sin(lam_im * dt)
    den = lam_re * lam_re + lam_im * lam_im
    nr = ab_re - 1.0
    coef_re = (nr * lam_re + ab_im * lam_im) / den
    coef_im = (ab_im * lam_re - nr * lam_im) / den
    bb_re = coef_re[..., None] * b_re - coef_im[..., None] * b_im
    bb_im = coef_re[..., None] * b_im + coef_im[..., None] * b_re
    bu_re = jnp.einsum('gpc,blgc->lbgp', bb_re, u)
    bu_im = jnp.einsum('gpc,blgc->lbgp', bb_im, u)
    bu_re = bu_re.at[0].add(ab_re * h0_re - ab_im * h0_im)
    bu_im = bu_im.at[0].add(ab_re * h0_im + ab_im * h0_re)
    a_re = jnp.broadcast_to(ab_re, bu_re.shape)
    a_im = jnp.broadcast_to(ab_im, bu_im.shape)

    def combine(e1, e2):
        a1r, a1i, b1r, b1i = e1
        a2r, a2i, b2r, b2i = e2
        return (a2r * a1r - a2i * a1i, a2r * a1i + a2i * a1r,
                a2r * b1r - a2i * b1i + b2r, a2r * b1i + a2i * b1r + b2i)

    _, _, h_re, h_im = lax.associative_scan(combine, (a_re, a_im, bu_re, bu_im), axis=0)
    y = (jnp.einsum('gcp,lbgp->blgc', c_re, h_re) - jnp.einsum('gcp,lbgp->blgc', c_im, h_im)
         + d_skip.reshape(S5_GROUPS, S5_GROUP) * u)
    return y, h_re[-1], h_im[-1]

def token_mixer(x, s_hg, s_re, s_im, lb, norm_g, w_in, onorm_g, w_branch_a, lam_re, lam_im, log_dt,
                b_re, b_im, c_re, c_im, d_skip, w_glu, b_glu, w_out):
    B, L, _ = x.shape
    h = rmsnorm(x, norm_g)
    proj = h @ w_in
    q, f_raw, i_in, o_gate, u, gate_a, gate_b = jnp.split(proj, IN_SPLITS, axis=-1)
    f = lb + (1.0 - lb) * jax.nn.sigmoid(f_raw)
    log_f = jnp.log(f)
    k = 1.0 - f
    o, s_hg_new = hgrn2_recurrence(
        (q * HG_SCALE).reshape(B, L, HG_HEADS, HG_DK), k.reshape(B, L, HG_HEADS, HG_DK),
        i_in.reshape(B, L, HG_HEADS, HG_DV), log_f.reshape(B, L, HG_HEADS, HG_DK),
        s_hg.astype(jnp.float32))
    o = o * lax.rsqrt(jnp.mean(o * o, axis=-1, keepdims=True) + RMS_EPS) * onorm_g
    o = o.reshape(B, L, HG_VW) * jax.nn.silu(o_gate)
    y_a = o @ w_branch_a
    y_s5, s_re_new, s_im_new = s5_branch(u.reshape(B, L, S5_GROUPS, S5_GROUP), s_re.astype(jnp.float32),
                                         s_im.astype(jnp.float32), lam_re, lam_im, log_dt,
                                         b_re, b_im, c_re, c_im, d_skip)
    z = jax.nn.gelu(y_s5.reshape(B, L, S5_WIDTH)) @ w_glu + b_glu
    za, zg = jnp.split(z, 2, axis=-1)
    y_b = za * jax.nn.sigmoid(zg)
    merged = jax.nn.sigmoid(gate_a) * y_a + jax.nn.sigmoid(gate_b) * y_b
    return merged @ w_out, s_hg_new, s_re_new, s_im_new

def hier_moe(h, w_rg, b_rg, w_re, b_re, w_gate, w_up, w_down):
    B, L, D = h.shape
    t = h.reshape(B * L, D)
    g_logits = (t @ w_rg + b_rg).astype(jnp.float32)
    g_prob = jax.nn.softmax(g_logits, axis=-1)
    g_idx = jnp.argmax(g_logits, axis=-1)
    g_w = jnp.take_along_axis(g_prob, g_idx[:, None], axis=-1)[:, 0]
    e_all = (jnp.einsum('td,gde->tge', t, w_re) + b_re).astype(jnp.float32)
    e_logits = jnp.take_along_axis(e_all, g_idx[:, None, None], axis=1)[:, 0]
    top_v, top_i = lax.top_k(e_logits, MOE_TOP_K)
    top_w = jax.nn.softmax(top_v, axis=-1) * g_w[:, None]
    expert_id = g_idx[:, None] * MOE_EXPERTS_PER_GROUP + top_i
    combine = jnp.einsum('tk,tke->te', top_w, jax.nn.one_hot(expert_id, N_EXPERTS, dtype=jnp.float32))
    y = jnp.zeros((B * L, D), jnp.float32)
    for e in range(N_EXPERTS):
        hid = jax.nn.silu(t @ w_gate[e]) * (t @ w_up[e])
        y = y + combine[:, e:e + 1] * (hid @ w_down[e])
    return y.reshape(B, L, D)

def setup_inputs(seed: int = 0) -> dict:
    key = jax.random.key(seed)
    ks = jax.random.split(key, 32)
    f32 = jnp.float32
    nrm = lambda k, shape, s: jax.random.normal(k, shape, f32) * s
    n_idx = jnp.arange(S5_STATE, dtype=f32)
    return {
        'x_prompt': nrm(ks[0], (BATCH, SEQ, D_MODEL), 1.0),
        'x_sample': nrm(ks[1], (DEC_BATCH, DEC_SEQ, D_MODEL), 1.0),
        'state_hgrn': nrm(ks[2], (DEPTH, DEC_BATCH, HG_HEADS, HG_DK, HG_DV), 0.5),
        'state_s5_re': nrm(ks[3], (DEPTH, DEC_BATCH, S5_GROUPS, S5_STATE), 0.5),
        'state_s5_im': nrm(ks[4], (DEPTH, DEC_BATCH, S5_GROUPS, S5_STATE), 0.5),
        'norm_mix_g': 1.0 + nrm(ks[5], (DEPTH, D_MODEL), 0.02),
        'w_in': nrm(ks[6], (DEPTH, D_MODEL, IN_WIDTH), D_MODEL ** -0.5),
        'hgrn_lb_raw': nrm(ks[7], (DEPTH + 1, HG_KW), 0.1),
        'hgrn_onorm_g': 1.0 + nrm(ks[8], (DEPTH, HG_HEADS, HG_DV), 0.02),
        'w_branch_a': nrm(ks[9], (DEPTH, HG_VW, D_MODEL), HG_VW ** -0.5),
        's5_lambda_re': -0.5 + nrm(ks[10], (DEPTH, S5_GROUPS, S5_STATE), 0.02),
        's5_lambda_im': math.pi * n_idx + nrm(ks[11], (DEPTH, S5_GROUPS, S5_STATE), 0.02),
        's5_log_dt': jax.random.uniform(ks[12], (DEPTH, S5_GROUPS), f32, math.log(S5_DT_MIN), math.log(S5_DT_MAX)),
        's5_b_re': nrm(ks[13], (DEPTH, S5_GROUPS, S5_STATE, S5_GROUP), (2 * S5_GROUP) ** -0.5),
        's5_b_im': nrm(ks[14], (DEPTH, S5_GROUPS, S5_STATE, S5_GROUP), (2 * S5_GROUP) ** -0.5),
        's5_c_re': nrm(ks[15], (DEPTH, S5_GROUPS, S5_GROUP, S5_STATE), (2 * S5_STATE) ** -0.5),
        's5_c_im': nrm(ks[16], (DEPTH, S5_GROUPS, S5_GROUP, S5_STATE), (2 * S5_STATE) ** -0.5),
        's5_d': nrm(ks[17], (DEPTH, S5_WIDTH), 1.0),
        'w_glu': nrm(ks[18], (DEPTH, S5_WIDTH, 2 * D_MODEL), S5_WIDTH ** -0.5),
        'b_glu': nrm(ks[19], (DEPTH, 2 * D_MODEL), 0.01),
        'w_out': nrm(ks[20], (DEPTH, D_MODEL, D_MODEL), D_MODEL ** -0.5),
        'norm_ffn_g': 1.0 + nrm(ks[21], (DEPTH, D_MODEL), 0.02),
        'w_router_group': nrm(ks[22], (DEPTH, D_MODEL, MOE_GROUPS), D_MODEL ** -0.5),
        'b_router_group': nrm(ks[23], (DEPTH, MOE_GROUPS), 0.01),
        'w_router_expert': nrm(ks[24], (DEPTH, MOE_GROUPS, D_MODEL, MOE_EXPERTS_PER_GROUP), D_MODEL ** -0.5),
        'b_router_expert': nrm(ks[25], (DEPTH, MOE_GROUPS, MOE_EXPERTS_PER_GROUP), 0.01),
        'w_exp_gate': nrm(ks[26], (DEPTH, N_EXPERTS, D_MODEL, D_EXPERT), D_MODEL ** -0.5),
        'w_exp_up': nrm(ks[27], (DEPTH, N_EXPERTS, D_MODEL, D_EXPERT), D_MODEL ** -0.5),
        'w_exp_down': nrm(ks[28], (DEPTH, N_EXPERTS, D_EXPERT, D_MODEL), D_EXPERT ** -0.5),
        'norm_final_g': 1.0 + nrm(ks[29], (D_MODEL,), 0.02),
    }

def reference(x_prompt, x_sample, state_hgrn, state_s5_re, state_s5_im, norm_mix_g, w_in, hgrn_lb_raw,
              hgrn_onorm_g, w_branch_a, s5_lambda_re, s5_lambda_im, s5_log_dt, s5_b_re, s5_b_im, s5_c_re,
              s5_c_im, s5_d, w_glu, b_glu, w_out, norm_ffn_g, w_router_group, b_router_group,
              w_router_expert, b_router_expert, w_exp_gate, w_exp_up, w_exp_down, norm_final_g):
    lb_all = jnp.cumsum(jax.nn.softmax(hgrn_lb_raw.astype(jnp.float32), axis=0), axis=0)

    def trunk(x, s_hg_all, s_re_all, s_im_all):
        h = x
        new_hg, new_re, new_im = [], [], []
        for l in range(DEPTH):
            mix, s_hg, s_re, s_im = token_mixer(
                h, s_hg_all[l], s_re_all[l], s_im_all[l], lb_all[l], norm_mix_g[l], w_in[l], hgrn_onorm_g[l],
                w_branch_a[l], s5_lambda_re[l], s5_lambda_im[l], s5_log_dt[l], s5_b_re[l], s5_b_im[l],
                s5_c_re[l], s5_c_im[l], s5_d[l], w_glu[l], b_glu[l], w_out[l])
            h = h + mix
            h = h + hier_moe(rmsnorm(h, norm_ffn_g[l]), w_router_group[l], b_router_group[l],
                             w_router_expert[l], b_router_expert[l], w_exp_gate[l], w_exp_up[l], w_exp_down[l])
            new_hg.append(s_hg)
            new_re.append(s_re)
            new_im.append(s_im)
        y = rmsnorm(h, norm_final_g).astype(x.dtype)
        return y, jnp.stack(new_hg), jnp.stack(new_re), jnp.stack(new_im)

    bp = x_prompt.shape[0]
    zero_hg = jnp.zeros((DEPTH, bp, HG_HEADS, HG_DK, HG_DV), jnp.float32)
    zero_s5 = jnp.zeros((DEPTH, bp, S5_GROUPS, S5_STATE), jnp.float32)
    y_prompt, hg_p, re_p, im_p = trunk(x_prompt, zero_hg, zero_s5, zero_s5)
    y_sample, hg_s, re_s, im_s = trunk(x_sample, state_hgrn, state_s5_re, state_s5_im)
    return (y_prompt, y_sample, hg_p, re_p, im_p, hg_s, re_s, im_s)


_drawn_inputs = setup_inputs


def setup_inputs(seed=0):
    import zlib

    import numpy as np

    out = dict(_drawn_inputs(seed))
    spreads = {}
    factors = {'hgrn_onorm_g': 3.016,
     'b_glu': 14.902,
     'b_router_group': 13.811,
     'b_router_expert': 10.681,
     'norm_final_g': 8.609,
     'norm_ffn_g': 3.16}
    for name, (base, spread) in spreads.items():
        noise = np.random.default_rng([zlib.crc32(name.encode()), seed]).standard_normal(out[name].shape)
        drawn = base * np.exp(spread * noise) if base else spread * noise
        out[name] = __import__('jax').numpy.asarray(drawn.astype(out[name].dtype))
    for name, factor in factors.items():
        out[name] = (out[name] * factor).astype(out[name].dtype)
    return out
```

```python
from contextlib import ExitStack

import numpy as np
import concourse.bass as bass
from concourse import mybir

F32 = mybir.dt.float32
I32 = mybir.dt.int32
U32 = mybir.dt.uint32
ALU = mybir.AluOpType
ACT = mybir.ActivationFunctionType
X = mybir.AxisListType.X

P = 128
D = 1024
KD = D // P
NP_TOK, NB, SEQ_S = 256, 8, 8
NS_TOK = NB * SEQ_S
NT = NP_TOK + NS_TOK
TOK = [(0, P), (P, P), (2 * P, NS_TOK)]
HEADS, CH = 8, 64
NCH = NP_TOK // CH
GH = 4
W4 = GH * P
HG_SCALE = float(P) ** -0.5
GROUPS_S5, ST, CG = 32, 64, 16
S5W = GROUPS_S5 * CG
T5 = GROUPS_S5 * ST // P
T5H = T5 // 2
NX, OFF_Q, OFF_F, OFF_V, OFF_O, OFF_U, OFF_GA, OFF_GB = 6656, 0, 1024, 2048, 3072, 4096, 4608, 5632
EPS = 1e-6
NG, NE_G = 4, 8
NE = NG * NE_G
DE = 512
KE = DE // P
CAP = 64
OV = 2 * NT // (CAP + 1)
Y_ROWS = NE * CAP + OV * CAP
UNIT = 4096
BIG = 3.0e38

UNITS = ["u", "f0", "q0", "v0", "f1", "q1", "v1", "o0", "o1", "wa0", "ga0", "wa1", "ga1", "za", "zg",
         "gb0", "gb1", "wo0", "wo1"]
MIX_SLOTS = 3
SLOT = {u: n % MIX_SLOTS for n, u in enumerate(UNITS)}
TURN = {u: n // MIX_SLOTS for n, u in enumerate(UNITS)}
USED = [sum(SLOT[u] == s for u in UNITS) for s in range(MIX_SLOTS)] + [1, 1, 1]
GATE_SLOT, UP_SLOT, DOWN_SLOT = [3, 4], [5, 1], [2, 0]


def schedule():
    steps = [("xt", i, h) for i in range(3) for h in range(2)] + [("params",)]
    steps += [("proj", "u", j) for j in range(4)] + [("proj", "f0", j) for j in range(4)]
    steps += [("h0",), ("bt", 0), ("bt", 1), ("ct", 0), ("ct", 1)]
    steps += [("proj", "q0", j) for j in range(4)] + [("proj", "v0", j) for j in range(3)]
    later = [("elem", 0)]
    later += [("proj", "f1", j) for j in range(4)]
    later += [("kn", 0, i) for i in range(3)] + [("sc", 0, i) for i in range(3)]
    later += [("proj", "q1", j) for j in range(2)] + [("ds", 0, c) for c in range(NCH)]
    later += [("proj", "q1", j) for j in range(2, 4)]
    for h in range(GH):
        later += [("o", 0, h)] + [("dss", 0, h, i) for i in range(2)]
    later += [("mean", 0, h) for h in range(GH)]
    later += [("proj", "v1", j) for j in range(3)] + [("elem", 1)]
    later += [("proj", "o0", j) for j in range(4)]
    later += [("kn", 1, i) for i in range(3)] + [("sc", 1, i) for i in range(3)]
    later += [("ds", 1, c) for c in range(NCH)]
    for h in range(GH):
        later += [("o", 1, h)] + [("dss", 1, h, i) for i in range(2)]
    later += [("mean", 1, h) for h in range(GH)]
    later += [("proj", "o1", j) for j in range(4)]
    for h in range(2):
        for j in range(4):
            later += [("proj", f"wa{h}", j), ("proj", f"ga{h}", j)]
    t = seen = 0
    for st in later:
        steps.append(st)
        seen += st[0] == "proj"
        if st[0] == "proj" and seen % 2 == 0 and t <= T5:
            if t < T5:
                steps.append(("bu", t))
            if t >= 1:
                steps.append(("sy", t - 1))
            t += 1
    while t <= T5:
        if t < T5:
            steps.append(("bu", t))
        if t >= 1:
            steps.append(("sy", t - 1))
        t += 1
    steps += [("states",)]
    for j in range(KD):
        steps += [("proj", "za", j), ("proj", "zg", j)]
    steps += [("proj", "gb0", j) for j in range(4)] + [("proj", "gb1", j) for j in range(4)]
    for h in range(2):
        steps += [("mix", h, i) for i in range(3)]
    steps += [("ht", i, h) for i in range(3) for h in range(2)] + [("logits", i) for i in range(3)]
    steps += [("rank",)]
    return steps


STEPS = schedule()


def banks():
    use = {"bu": None, "sy": 4, "kn": None, "sc": None, "o": None, "mean": 7, "ds": 7, "dss": 7}
    taken, where, turn56, turn01 = [0] * 8, {}, 0, 0

    def take(key, b):
        where[key] = (b, taken[b])
        taken[b] += 1

    for st in STEPS:
        if st[0] in ("elem",):
            continue
        if st[0] == "bu":
            take(("bur",) + st[1:], 2)
            take(("bui",) + st[1:], 3)
        elif st[0] == "sy":
            if st[1] % 4 == 0:
                take(("y5", st[1] // 4), 4)
        elif st[0] == "states":
            take(("fs",), 5)
            take(("fss",), 6)
        elif st[0] in ("kn", "sc", "o"):
            take(st, 5 + turn56 % 2)
            turn56 += 1
        elif st[0] in ("mean", "ds", "dss"):
            take(st, 7)
        else:
            take(st, turn01 % 2)
            turn01 += 1
    return where


BANK = banks()
UNIT_LAST = {}
for _st in STEPS:
    if _st[0] == "proj":
        UNIT_LAST[_st[1]] = _st
    if _st[0] == "mix":
        UNIT_LAST[f"wo{_st[1]}"] = _st


def mixer_moe(nc, a, o):
    ctx = ExitStack()
    with ctx:
        def sb(name, shape, dt=F32):
            return ctx.enter_context(nc.sbuf_tensor(name, shape, dt))

        def sem(name):
            return ctx.enter_context(nc.semaphore(name))

        y_dram = nc.dram_tensor("expert_rows", (Y_ROWS, D), F32, kind="Internal").ap()

        K = 256
        arena = sb("arena", [P, 191 * K])

        def part(kib, n, pat=None, rows=P, **kw):
            v = arena[0:rows, int(kib * K):int(kib * K) + n]
            return v.rearrange(pat, **kw) if pat else v

        ring = [part(k, UNIT) for k in (0, 16, 32, 60, 76, 92)]
        h2 = part(48, 3 * D, "p (t d) -> p t d", t=3)
        kk = part(60, GH * NT, "p (h n) -> p h n", h=GH)
        junk = part(60, D)
        bc = part(65, GH * NT, "p (h n) -> p h n", h=GH)
        eb = part(70, GH * NT, "p (h n) -> p h n", h=GH)
        kd = part(75, GH * NT, "p (h n) -> p h n", h=GH)
        qd = part(80, GH * NT, "p (h n) -> p h n", h=GH)
        sp_ = part(85, NCH * W4, "p (c n) -> p c n", c=NCH)
        stt_ = part(93, 2 * NB * P, "p (s b v) -> p s b v", s=2, b=NB)
        scp = part(101, 2 * GH * P, "p (c h t) -> p c h t", h=GH, c=2)
        scs = part(124, GH * NS_TOK, "p (h t) -> p h t", rows=NS_TOK, h=GH)
        blast = part(107.5, GH * 12, "p (h c) -> p h c", h=GH)
        eblast = part(107.75, GH * 12, "p (h c) -> p h c", h=GH)
        rstd_o = part(105, NT)
        osq = part(106.25, NT)
        vn = part(108, 3 * W4, "p (t n) -> p t n", t=3)
        kn = part(114, 3 * W4, "p (t n) -> p t n", t=3)
        vm = part(120, NB * P, "p (b v) -> p b v", rows=NS_TOK, b=NB)
        rows76 = part(108, P)
        braw = part(108.5, 2 * T5 * CG, "p (r t c) -> p r t c", r=2, t=T5)
        craw = part(110.5, 2 * 4 * ST, "p (r t s) -> p r t s", r=2, t=4)
        h0rows = part(112.5, 2 * P, "p (r s) -> p r s", r=2)
        h0t = part(113.5, 2 * P, "p (r b t) -> p r t b", r=2, b=NB)
        bd = part(114.5, 2 * T5 * 2 * CG, "p (r t q c) -> p r t q c", r=2, t=T5, q=2)
        cd = part(118.5, 2 * 4 * P, "p (r t q s) -> p r t q s", r=2, t=4, q=2)
        ptmp = part(122.5, T5 * CG, "p (t c) -> p t c", t=T5)
        ptmp2 = part(123.5, T5 * CG, "p (t c) -> p t c", t=T5)
        smask = part(125, NT)
        cosT = part(127, T5H * NT, "p (t n) -> p t n", t=T5H)
        sinT = part(137, T5H * NT, "p (t n) -> p t n", t=T5H)
        wr, wi, tm1, tm2 = (part(147 + 1.25 * i, NT) for i in range(4))
        gr = part(152, 2 * NT, "p (s n) -> p s n", s=2)
        gi = part(154.5, 2 * NT, "p (s n) -> p s n", s=2)
        hr = part(157, 2 * NT, "p (s n) -> p s n", s=2)
        hi = part(159.5, 2 * NT, "p (s n) -> p s n", s=2)
        pt1, pt2, rdec = (part(162 + 1.25 * i, NT) for i in range(3))
        ptab = part(162, T5H * P)
        fstage = part(152, 2 * P, "p (r s) -> p r s", r=2)
        zrow = part(127, D, rows=CAP)
        hT = part(166, KD * NT, "p (k n) -> p k n", k=KD)
        oT = part(176, KD * NT, "p (k n) -> p k n", k=KD)
        uT = part(186, 4 * NT, "p (k n) -> p k n", k=4)
        gy = uT
        xn = part(176, 2 * D, "p (s d) -> p s d", s=2)
        grow = part(186, D)
        merged = part(108, KD * NT, "p (k n) -> p k n", k=KD)
        sga = part(118, 2 * NT, "p (s n) -> p s n", s=2)
        hn = part(108, 3 * D, "p (t d) -> p t d", t=3)
        pick = part(120.5, 3 * P, "p (t s) -> p t s", t=3)
        xT = part(122, KD * P, "p (k s) -> p k s", k=KD)
        sil = part(126, DE)
        hid = part(128, DE)
        hidT = part(130, DE, "p (k s) -> p k s", k=KE)
        yrow = part(132, D, "p (h d) -> p h d", h=2)
        gffn = part(138, D)
        gfin = part(142, D)
        ya = part(146, 2 * D, "p (s d) -> p s d", s=2)
        yb = part(154, 2 * D, "p (s d) -> p s d", s=2)
        hnT = part(146, KD * NT, "p (k n) -> p k n", k=KD)
        wrt = part(156, KD * (NG + NE), "p (k e) -> p k e", k=KD)
        brt = part(158, NG + NE)
        lg = part(168, 3 * 36, "p (t e) -> p t e", t=3)
        r32 = [part(169 + i, 3 * NE, "p (t g e) -> p t g e", t=3, g=NG) for i in range(8)]
        r8 = [part(177 + 0.25 * i, 3 * NE_G, "p (t e) -> p t e", t=3) for i in range(12)]
        r1 = [part(181 + 0.0625 * i, 3, "p (t e) -> p t e", t=3) for i in range(16)]
        ovj = part(183, OV * NE, "p (j e) -> p j e", j=OV)
        nE = part(185, NE)
        ovt = part(185.25, NE)
        incl = part(185.5, NE)
        corr = part(185.75, NE)
        ident = sb("ident", [P, P])
        ones = sb("ones", [P, P])
        upper = sb("upper", [P, P])
        iota_s = sb("iota_s", [P, P])
        iota_i = sb("iota_i", [P, P], I32)
        par_i = sb("par_i", [P, 2], I32)
        par = sb("par", [P, 2])
        negp = sb("negp", [P, 2])
        cmask = sb("cmask", [P, NT])
        seqm = sb("seqm", [NS_TOK, NB])
        rev = sb("rev", [P, NE])
        pcol = sb("pcol", [P, 76])
        ldt = sb("ldt", [P, GROUPS_S5])
        cf = sb("cf", [P, 24, T5])
        lb = sb("lb", [P, 6, HEADS])
        ah = sb("ah", [P, 2, T5, NB])
        fsp = sb("fsp", [P, 2, T5])
        fss = sb("fss", [P, 2, NB, T5])
        btr = sb("btr", [P, 2, 4, P])
        ctr = sb("ctr", [P, 2, 4, P])
        ss = sb("ss", [P, 3])
        epsc = sb("epsc", [P, 1])
        slot = sb("slot", [P, 2, 3])
        wtop = sb("wtop", [P, 2, 3])
        sidx = sb("sidx", [P, 3, 2], I32)
        ovi = sb("ovi", [P, 16], I32)

        LBH, OML, NOML, ON, ONG = 0, 1, 2, 3, 4

        ps = [ctx.enter_context(nc.psum_tensor(f"bank{i}", [P, 512], F32)) for i in range(8)]
        x_in = sem("x_in")
        gmix_in = sem("gmix_in")
        small_in = sem("small_in")
        late_in = sem("late_in")
        st_in = [sem(f"st_in{i}") for i in range(2)]
        st_out = [sem(f"st_out{i}") for i in range(2)]
        full = [sem(f"unit_full{i}") for i in range(6)]
        used = [sem(f"unit_used{i}") for i in range(6)]
        filled = [sem(f"bank_filled{i}") for i in range(8)]
        emptied = [sem(f"bank_emptied{i}") for i in range(8)]
        names = ["consts", "cp_done", "ss_done", "zeroed", "rstd_done", "xn_done", "dt_exp", "mag_exp", "mag_in", "phasor", "lb_in", "lb_exp",
                 "lb_done", "bdcd", "tab_done", "k_done", "logf", "scan_done", "exp_done", "diff_done", "dexp", "kd_done",
                 "qd_done", "kl_done", "kn_done", "sc_raw", "sc_done", "state_new", "o_raw", "vm_done", "vm_used",
                 "st_scaled", "st_sum", "g_done", "g_used", "h_done", "h_used", "y5_ev", "gy_done", "v_done",
                 "sq_done", "o_final", "sig_a", "sig_g", "sil_o", "sig_used", "yb_sig", "merged_ok", "yb_done", "u_done", "fs_done", "fst_done",
                 "out_done", "h2_done", "ss2", "hn_done", "hnT_done", "mats", "rk_done", "gexp_in", "gexp", "slots",
                 "pick_done", "xT_done", "sel_done", "on_done", "f_done", "q_done",
                 "fin_ss", "fin_done", "y_out", "dve", "pool", "act", "tab_free", "h_fs",
                 "ov_w", "ov_p", "ov_sel", "ov_x", "ov_g", "ov_u", "ov_sil", "ov_hid", "ov_dn", "ov_y", "ov_st", "ov_t", "ov_hidT",
                 "silu_done", "hid_done", "hidT_ready", "hidT_done", "y_half", "y_copied"]
        S = {n: sem(n) for n in names}
        gathered = [sem(f"gathered{i}") for i in range(2)]
        y_stored = [sem(f"y_stored{e}") for e in range(2)]

        x_tok = [a["x_prompt"][0, 0:P, :], a["x_prompt"][0, P:2 * P, :],
                 a["x_sample"].rearrange("b s d -> (b s) d")]
        w_in = a["w_in"][0]
        sthg = a["state_hgrn"][0]

        def bcast_rows(v, n):
            return v.rearrange("(o d) -> o d", o=1).broadcast_to([n, v.shape[0]])

        def unit_src(u):
            if u in ("wo0", "wo1"):
                c = 512 * int(u[2])
                return a["w_out"][0][:, c:c + 512].rearrange("(k p) n -> p k n", p=P)
            if u in ("wa0", "wa1"):
                c = 512 * int(u[2])
                return a["w_branch_a"][0][:, c:c + 512].rearrange("(k p) n -> p k n", p=P)
            if u in ("za", "zg"):
                c = D * (u == "zg")
                return a["w_glu"][0][:, c:c + D].rearrange("(k p) n -> p k n", p=P)
            base = {"u": OFF_U, "f0": OFF_F, "q0": OFF_Q, "v0": OFF_V, "f1": OFF_F + 512, "q1": OFF_Q + 512,
                    "v1": OFF_V + 512, "o0": OFF_O, "o1": OFF_O + 512, "ga0": OFF_GA, "ga1": OFF_GA + 512,
                    "gb0": OFF_GB, "gb1": OFF_GB + 512}[u]
            return w_in[:, base:base + 512].rearrange("(k p) n -> p k n", p=P)

        def unit_view(u, kt=KD):
            return ring[SLOT[u]].rearrange("p (k n) -> p k n", k=4 if u in ("za", "zg") else KD)

        wg_d, wu_d, wd_d = a["w_exp_gate"][0], a["w_exp_up"][0], a["w_exp_down"][0]

        def bank(key, n=512, rows=P):
            return ps[BANK[key][0]][0:rows, 0:n]

        def wait_filled(eng, key):
            b, n = BANK[key]
            eng.wait_ge(filled[b], n + 1)

        def wait_emptied(eng, key):
            b, n = BANK[key]
            if n:
                eng.wait_ge(emptied[b], n)

        def is_filled(ins, key):
            ins.then_inc(filled[BANK[key][0]], 1)

        def is_emptied(ins, key):
            ins.then_inc(emptied[BANK[key][0]], 1)

        def bt(v, n, at=None):
            return v.unsqueeze(len(v.shape)).broadcast_to(list(v.shape) + [n])

        block = ctx.enter_context(nc.Block())

        @block.sync
        def _(sp):
            for i, (t0, n) in enumerate(TOK):
                sp.dma_start(h2[0:n, i, :], x_tok[i]).then_inc(x_in, 16)
                if i == 0:
                    sp.dma_start(grow, bcast_rows(a["norm_mix_g"][0], P)).then_inc(gmix_in, 16)
            heads = 0

            def states_in(h):
                if h >= 2:
                    sp.wait_ge(st_out[h % 2], 16 * (h // 2))
                sp.dma_start(stt_[:, h % 2, :, :], sthg[:, h, :, :].rearrange("b k v -> k b v")).then_inc(
                    st_in[h % 2], 16)

            def states_out(h):
                sp.wait_ge(S["st_sum"], 2 * h + 2)
                sp.dma_start(o["hg_s"][0, :, h, :, :].rearrange("b k v -> k b v"), stt_[:, h % 2, :, :]).then_inc(
                    st_out[h % 2], 16)

            for n, u in enumerate(UNITS):
                if TURN[u]:
                    sp.wait_ge(used[SLOT[u]], TURN[u])
                sp.dma_start(ring[SLOT[u]].rearrange("p (k n) -> p k n", k=4 if u in ("za", "zg") else KD),
                             unit_src(u)).then_inc(full[SLOT[u]], 16)
                if u == "q0":
                    states_in(0)
                    states_in(1)
                if u == "o1":
                    for h in range(0, GH):
                        states_out(h)
                        states_in(h + 2)
                    sp.wait_ge(S["state_new"], NCH)
                    sp.dma_start(o["hg_p"][0, 0, 0:GH].rearrange("h k v -> k h v"),
                                 sp_[:, NCH - 1, :].rearrange("p (h v) -> p h v", h=GH)).then_inc(S["out_done"], 16)
                if u == "ga0":
                    for h in range(GH, HEADS):
                        states_out(h)
                        if h + 2 < HEADS:
                            states_in(h + 2)
                    sp.wait_ge(S["state_new"], 2 * NCH)
                    sp.dma_start(o["hg_p"][0, 0, GH:HEADS].rearrange("h k v -> k h v"),
                                 sp_[:, NCH - 1, :].rearrange("p (h v) -> p h v", h=GH)).then_inc(S["out_done"], 16)
            sp.wait_ge(S["h_used"], T5)
            sp.wait_ge(S["fs_done"], T5)
            sp.dma_start(wrt[:, :, 0:NG], a["w_router_group"][0].rearrange("(p k) e -> p k e", p=P)).then_inc(late_in, 16)
            for g in range(NG):
                sp.dma_start(wrt[:, :, NG + NE_G * g:NG + NE_G * (g + 1)],
                             a["w_router_expert"][0, g].rearrange("(p k) e -> p k e", p=P)).then_inc(late_in, 16)
            sp.dma_start(brt[:, 0:NG], bcast_rows(a["b_router_group"][0], P)).then_inc(late_in, 16)
            sp.dma_start(brt[:, NG:], bcast_rows(a["b_router_expert"][0].rearrange("g e -> (g e)"), P)).then_inc(late_in, 16)
            sp.dma_start(gffn, bcast_rows(a["norm_ffn_g"][0], P)).then_inc(late_in, 16)
            sp.dma_start(gfin, bcast_rows(a["norm_final_g"], P)).then_inc(late_in, 16)
            for h in (HEADS - 2, HEADS - 1):
                sp.wait_ge(st_out[h % 2], 16 * (h // 2 + 1))
            sp.wait_ge(S["out_done"], 32)
            sp.wait_ge(S["o_final"], HEADS)
            with sp.Fori(0, NE // 2) as it:
                for slots, src in ((GATE_SLOT, wg_d), (UP_SLOT, wu_d), (DOWN_SLOT, wd_d)):
                    for e, s in enumerate(slots):
                        sp.wait_ge(used[s], it + USED[s])
                        sp.dma_start(ring[s], src[bass.ds(it * 2 + e, 1), :, :].rearrange(
                            "o (p k) n -> p (o k n)", p=P)).then_inc(full[s], 16)
            sp.wait_ge(S["slots"], 1)
            n_ov = sp.value_load(ovi[0:1, 15:16], min_val=0, max_val=OV)
            with sp.If(n_ov > 0):
                for s in range(3):
                    sp.wait_ge(used[s], USED[s] + NE // 2)
                with sp.Fori(0, n_ov) as j:
                    sp.wait_ge(S["ov_dn"], j + 1)
                    ex = sp.value_load(ovi[0:1, bass.ds(j, 1)], min_val=0, max_val=NE - 1)
                    for s, src in enumerate((wg_d, wu_d, wd_d)):
                        sp.dma_start(ring[s], src[bass.ds(ex, 1), :, :].rearrange(
                            "o (p k) n -> p (o k n)", p=P)).then_inc(S["ov_w"], 16)
            for i, (t0, n) in enumerate(TOK):
                sp.wait_ge(S["fin_done"], i + 1)
                dst = o["y_p"][0, t0:t0 + n, :] if i < 2 else o["y_s"].rearrange("b s d -> (b s) d")
                sp.dma_start(dst, h2[0:n, i, :]).then_inc(S["y_out"], 16)
            sp.wait_ge(S["y_out"], 48)
            sp.wait_ge(S["fst_done"], 6 * 16)

        @block.tensor
        def _(pe):
            mm = nc.tensor.matmul
            pe.wait_ge(S["consts"], 1)
            s5_waited = False
            for st in STEPS:
                kind = st[0]
                if kind == "elem":
                    continue
                if kind == "params":
                    pe.wait_ge(small_in, 13 * 16)
                    wait_emptied(pe, st)
                    is_filled(nc.tensor.transpose(bank(st, 76), rows76[0:76, :], ident[0:76, 0:76]), st)
                elif kind in ("xt", "ht"):
                    _, i, h = st
                    n = TOK[i][1]
                    pe.wait_ge(S["xn_done" if kind == "xt" else "hn_done"], i + 1)
                    wait_emptied(pe, st)
                    src = xn[:, i % 2, :] if kind == "xt" else hn[:, i, :]
                    for k in range(4):
                        c = (4 * h + k) * P
                        last = nc.tensor.transpose(ps[BANK[st][0]][:, k * n:(k + 1) * n], src[0:n, c:c + P],
                                                   ident[0:n, 0:n])
                    is_filled(last, st)
                elif kind == "h0":
                    wait_emptied(pe, st)
                    for r in range(2):
                        last = nc.tensor.transpose(ps[BANK[st][0]][:, r * P:(r + 1) * P], h0rows[:, r, :], ident[:, :])
                    is_filled(last, st)
                elif kind in ("bt", "ct"):
                    r = st[1]
                    pe.wait_ge(S["bdcd"], 2 if kind == "bt" else 4)
                    wait_emptied(pe, st)
                    for T in range(4):
                        src = bd[:, r, 4 * T:4 * T + 4, :, :].rearrange("p t q c -> p (t q c)") if kind == "bt" else \
                            cd[:, r, T, :, :].rearrange("p q s -> p (q s)")
                        last = nc.tensor.transpose(ps[BANK[st][0]][:, T * P:(T + 1) * P], src, ident[:, :])
                    is_filled(last, st)
                elif kind == "proj":
                    _, u, j = st
                    pe.wait_ge(full[SLOT[u]], 16 * (TURN[u] + 1))
                    wait_emptied(pe, st)
                    w = unit_view(u)
                    kt = 4 if u in ("za", "zg") else KD
                    if u == "u" and j == 0:
                        pe.wait_ge(S["cp_done"], 6)
                    if u == "wa0" and j == 0:
                        pe.wait_ge(S["o_final"], HEADS)
                    if u == "za" and j == 0:
                        pe.wait_ge(S["gy_done"], 4)
                    act = {"wa": oT, "za": gy, "zg": gy}.get(u[0:2], hT)
                    if u[0] == "v":
                        t0, n = TOK[j]
                        for k in range(kt):
                            last = mm(bank(st, 512, n), hT[:, k, t0:t0 + n], w[:, k, :], start=k == 0, stop=k == kt - 1)
                    else:
                        for k in range(kt):
                            last = mm(bank(st, NT), w[:, k, j * P:(j + 1) * P], act[:, k, :], start=k == 0,
                                      stop=k == kt - 1)
                    is_filled(last, st)
                    if UNIT_LAST[u] == st:
                        pe.wait_ge(filled[BANK[st][0]], BANK[st][1] + 1)
                        pe.sem_inc(used[SLOT[u]], 1)
                elif kind == "bu":
                    t = st[1]
                    if not s5_waited:
                        pe.wait_ge(S["u_done"], 4)
                        pe.wait_ge(S["bdcd"], 8)
                        s5_waited = True
                    for r, key in enumerate((("bur", t), ("bui", t))):
                        wait_emptied(pe, key)
                        j = 32 * (t % 4)
                        is_filled(mm(bank(key, NT), btr[j:j + 32, r, t // 4, :], uT[j:j + 32, t // 4, :],
                                     start=True, stop=True), key)
                elif kind == "sy":
                    t = st[1]
                    key = ("y5", t // 4)
                    if t % 4 == 0:
                        wait_emptied(pe, key)
                    pe.wait_ge(S["h_done"], t + 1)
                    j = 32 * (t % 4)
                    mm(ps[4][j:j + 32, 0:NT], ctr[:, 0, t // 4, j:j + 32], hr[:, t % 2, :], start=True, stop=False)
                    last = mm(ps[4][j:j + 32, 0:NT], ctr[:, 1, t // 4, j:j + 32], hi[:, t % 2, :], start=False, stop=True)
                    last.then_inc(S["h_used"], 1)
                elif kind == "kn":
                    _, g, i = st
                    t0, n = TOK[i]
                    pe.wait_ge(S["kl_done"], g + 1)
                    wait_emptied(pe, st)
                    for h in range(GH):
                        last = nc.tensor.transpose(ps[BANK[st][0]][0:n, h * P:(h + 1) * P], bc[:, h, t0:t0 + n], ident[:, :])
                    is_filled(last, st)
                elif kind == "sc":
                    _, g, i = st
                    wait_emptied(pe, st)
                    pe.wait_ge(S["qd_done"], g + 1)
                    pe.wait_ge(S["kd_done"], g + 1)
                    b = ps[BANK[st][0]]
                    for h in range(GH):
                        if i < 2:
                            last = mm(b[:, h * P:(h + 1) * P], kd[:, h, i * P:(i + 1) * P], qd[:, h, i * P:(i + 1) * P],
                                      start=True, stop=True)
                        else:
                            last = mm(b[0:NS_TOK, h * NS_TOK:(h + 1) * NS_TOK], kd[:, h, NP_TOK:NT], qd[:, h, NP_TOK:NT],
                                      start=True, stop=True)
                    is_filled(last, st)
                elif kind == "ds":
                    _, g, c = st
                    wait_emptied(pe, st)
                    pe.wait_ge(S["kn_done"], 3 * (g + 1))
                    pe.wait_ge(S["v_done"], 3 * (g + 1))
                    r = CH * (c % 2)
                    for h in range(GH):
                        last = mm(ps[7][:, h * P:(h + 1) * P], kn[r:r + CH, c // 2, h * P:(h + 1) * P],
                                  vn[r:r + CH, c // 2, h * P:(h + 1) * P], start=True, stop=True)
                    is_filled(last, st)
                elif kind == "dss":
                    _, g, h, i = st
                    wait_emptied(pe, st)
                    pe.wait_ge(S["vm_done"], GH * g + h + 1)
                    is_filled(mm(bank(st), kn[0:NS_TOK, 2, h * P:(h + 1) * P],
                                 vm[:, 4 * i:4 * i + 4, :].rearrange("p b v -> p (b v)"), start=True, stop=True), st)
                elif kind == "o":
                    _, g, h = st
                    wait_emptied(pe, st)
                    pe.wait_ge(S["sc_done"], 3 * (g + 1))
                    pe.wait_ge(S["state_new"], NCH * (g + 1))
                    pe.wait_ge(st_in[h % 2], 16 * ((GH * g + h) // 2 + 1))
                    b = ps[BANK[st][0]]
                    for c in range(2):
                        mm(b[:, c * P:(c + 1) * P], vn[:, c, h * P:(h + 1) * P], scp[:, c, h, :], start=True, stop=True)
                        for cc in range(max(2 * c, 1), 2 * c + 2):
                            s = CH * cc
                            mm(b[:, s:s + CH], sp_[:, cc - 1, h * P:(h + 1) * P], qd[:, h, s:s + CH], start=False,
                               stop=True, skip_group_check=True)
                    mm(b[:, NP_TOK:NT], vn[0:NS_TOK, 2, h * P:(h + 1) * P], scs[:, h, :], start=True, stop=True)
                    for q in range(NB):
                        s = NP_TOK + SEQ_S * q
                        last = mm(b[:, s:s + SEQ_S], stt_[:, h % 2, q, :], qd[:, h, s:s + SEQ_S], start=False,
                                  stop=True, skip_group_check=True)
                    is_filled(last, st)
                elif kind == "mean":
                    _, g, h = st
                    wait_emptied(pe, st)
                    pe.wait_ge(S["sq_done"], GH * g + h + 1)
                    is_filled(mm(bank(st, NT), ones[:, :], osq, start=True, stop=True), st)
                elif kind == "states":
                    pe.wait_ge(S["fs_done"], T5)
                    for key, n in ((("fs",), 1), (("fss",), NB)):
                        wait_emptied(pe, key)
                        for r in range(2):
                            src = fsp[:, r, :] if n == 1 else fss[:, r].rearrange("p b t -> p (b t)")
                            if n == 1:
                                last = nc.tensor.transpose(ps[BANK[key][0]][0:T5, r * P:(r + 1) * P], src, ident[:, :])
                            else:
                                last = nc.tensor.transpose(ps[BANK[key][0]][:, r * P:(r + 1) * P], src, ident[:, :])
                        is_filled(last, key)
                elif kind == "mix":
                    _, h, i = st
                    u = f"wo{h}"
                    t0, n = TOK[i]
                    pe.wait_ge(full[SLOT[u]], 16 * (TURN[u] + 1))
                    wait_emptied(pe, st)
                    pe.wait_ge(S["merged_ok"], 3 * KD)
                    w = unit_view(u)
                    for k in range(KD):
                        last = mm(bank(st, 512, n), merged[:, k, t0:t0 + n], w[:, k, :], start=k == 0, stop=k == KD - 1)
                    is_filled(last, st)
                    if i == 2:
                        pe.wait_ge(filled[BANK[st][0]], BANK[st][1] + 1)
                        pe.sem_inc(used[SLOT[u]], 1)
                elif kind == "logits":
                    i = st[1]
                    t0, n = TOK[i]
                    pe.wait_ge(late_in, 9 * 16)
                    pe.wait_ge(S["hnT_done"], 6)
                    wait_emptied(pe, st)
                    for k in range(KD):
                        last = mm(bank(st, NG + NE, n), hnT[:, k, t0:t0 + n], wrt[:, k, :], start=k == 0, stop=k == KD - 1)
                    is_filled(last, st)
                elif kind == "rank":
                    pe.wait_ge(S["mats"], 1)
                    wait_emptied(pe, st)
                    M = r32[2]
                    b = ps[BANK[st][0]]
                    for i in range(4):
                        for j in range(min(i, 3)):
                            last = mm(b[:, NE * i:NE * (i + 1)], ones[:, :], M[:, j].rearrange("p g e -> p (g e)"),
                                      start=j == 0, stop=i == 3 and j == 2)
                        if i < 3:
                            last = mm(b[:, NE * i:NE * (i + 1)], upper[:, :], M[:, i].rearrange("p g e -> p (g e)"),
                                      start=i == 0, stop=True)
                    is_filled(last, st)
                if kind == "rank":
                    break

            def select(width):
                for k in range(KD):
                    for i, (t0, n) in enumerate(TOK):
                        last = mm(ps[k // 4][:, (k % 4) * P:(k % 4) * P + width], hn[0:n, i, k * P:(k + 1) * P],
                                  pick[0:n, i, 0:width], start=i == 0, stop=i == 2)
                return last

            for s in (3, 4, 5):
                pe.sem_inc(used[s], 1)
            pe.wait_ge(emptied[BANK[("rank",)][0]], BANK[("rank",)][1] + 1)
            pe.wait_ge(S["pick_done"], 1)
            select(P).then_inc(S["sel_done"], 1)
            with pe.Fori(0, NE // 2) as it:
                pe.wait_ge(S["xT_done"], it + 1)
                for slots, b in ((GATE_SLOT, 2), (UP_SLOT, 3)):
                    for s in slots:
                        pe.wait_ge(full[s], it * 16 + 16 * (USED[s] + (s < 3)))
                    pe.wait_ge(S["hid_done"], it + 1)
                    for k in range(KD):
                        for e, s in enumerate(slots):
                            last = mm(ps[b][e * CAP:(e + 1) * CAP, :], xT[:, k, e * CAP:(e + 1) * CAP],
                                      ring[s][:, k * DE:(k + 1) * DE], start=k == 0, stop=k == KD - 1)
                            if k == KD - 1:
                                last.then_inc(used[s], 1)
                pe.wait_ge(S["pick_done"], it + 2)
                select(P).then_inc(S["sel_done"], 1)
                pe.wait_ge(S["hid_done"], it + 2)
                pe.wait_ge(S["hidT_done"], it + 1)
                for m in range(KE):
                    last = nc.tensor.transpose(ps[4][:, m * P:(m + 1) * P], hid[:, m * P:(m + 1) * P], ident[:, :])
                last.then_inc(S["hidT_ready"], 1)
                for s in DOWN_SLOT:
                    pe.wait_ge(full[s], it * 16 + 16 * (USED[s] + (s < 3)))
                pe.wait_ge(S["hidT_done"], it + 2)
                pe.wait_ge(S["y_copied"], it + 1)
                for h in range(2):
                    for k in range(KE):
                        for e, s in enumerate(DOWN_SLOT):
                            last = mm(ps[6 + h][e * CAP:(e + 1) * CAP, :], hidT[:, k, e * CAP:(e + 1) * CAP],
                                      ring[s][:, k * D + 512 * h:k * D + 512 * (h + 1)], start=k == 0, stop=k == KE - 1)
                            if h == 1 and k == KE - 1:
                                last.then_inc(used[s], 1)
            n_ov = pe.value_load(ovi[0:1, 15:16], min_val=0, max_val=OV)
            with pe.If(n_ov > 0):
                pe.wait_ge(S["xT_done"], NE // 2 + 1)
                pe.wait_ge(S["y_copied"], NE // 2 + 1)
                pe.sem_inc(S["ov_dn"], 1)
                with pe.Fori(0, n_ov) as j:
                    pe.wait_ge(S["ov_p"], j + 1)
                    select(CAP).then_inc(S["ov_sel"], 1)
                    pe.wait_ge(S["ov_x"], j + 1)
                    pe.wait_ge(S["ov_w"], j * 48 + 48)
                    for w, name in enumerate(("ov_g", "ov_u")):
                        for k in range(KD):
                            last = mm(ps[2 + w][0:CAP, :], xT[:, k, 0:CAP], ring[w][:, k * DE:(k + 1) * DE],
                                      start=k == 0, stop=k == KD - 1)
                        last.then_inc(S[name], 1)
                    pe.wait_ge(S["ov_hid"], j + 1)
                    for m in range(KE):
                        last = nc.tensor.transpose(ps[4][:, m * P:(m + 1) * P], hid[:, m * P:(m + 1) * P], ident[:, :])
                    last.then_inc(S["ov_t"], 1)
                    pe.wait_ge(S["ov_hidT"], j + 1)
                    for h in range(2):
                        for k in range(KE):
                            last = mm(ps[6 + h][0:CAP, :], hidT[:, k, 0:CAP],
                                      ring[2][:, k * D + 512 * h:k * D + 512 * (h + 1)], start=k == 0, stop=k == KE - 1)
                    last.then_inc(S["ov_dn"], 1)

        @block.scalar
        def _(act):
            ac = nc.scalar.activation
            cnt = [0]

            def link(ins):
                cnt[0] += 1
                ins.then_inc(S["act"], 1)
                act.wait_ge(S["act"], cnt[0])

            def rsqrt_mean(squares, v, width, done):
                link(squares)
                link(ac(v, v, ACT.Ln, scale=1.0 / width, bias=epsc[0:v.shape[0], :]))
                ac(v, v, ACT.Exp, scale=-0.5).then_inc(done, 1)

            dm = lambda dst, src: act.dma_start(dst, src).then_inc(small_in, 16)
            dm(rows76[0:16, :], a["hgrn_lb_raw"].rearrange("r (h k) -> (r h) k", k=P))
            dm(rows76[16:24, :], a["hgrn_onorm_g"][0])
            dm(rows76[24:40, :], a["b_glu"][0].rearrange("(h k) -> h k", k=P))
            dm(rows76[40:44, :], a["s5_d"][0].rearrange("(h k) -> h k", k=P))
            dm(rows76[44:60, :], a["s5_lambda_re"][0].rearrange("(t q) s -> t (q s)", q=2))
            dm(rows76[60:76, :], a["s5_lambda_im"][0].rearrange("(t q) s -> t (q s)", q=2))
            dm(ldt[:, :], bcast_rows(a["s5_log_dt"][0], P))
            for r, nme in enumerate(("s5_b_re", "s5_b_im")):
                dm(braw[:, r], a[nme][0].rearrange("(t q) s c -> (q s) t c", q=2))
            for r, nme in enumerate(("s5_c_re", "s5_c_im")):
                dm(craw[:, r], a[nme][0].rearrange("(t g) c s -> (g c) t s", t=4))
            for r, nme in enumerate(("state_s5_re", "state_s5_im")):
                dm(h0rows[:, r], a[nme][0].rearrange("b (t q) s -> (b t) (q s)", q=2))
            for i, (t0, n) in enumerate(TOK):
                act.wait_ge(x_in, 48)
                if i == 0:
                    act.wait_ge(S["consts"], 1)
                rsqrt_mean(ac(junk[0:n, :], h2[0:n, i, :], ACT.Square, accum_out=ss[0:n, i:i + 1]),
                           ss[0:n, i:i + 1], D, S["ss_done"])
            act.wait_ge(small_in, 13 * 16)
            for q in range(2):
                ac(cf[ST * q:ST * (q + 1), 0, :], ldt[ST * q:ST * (q + 1), q:GROUPS_S5:2], ACT.Exp).then_inc(S["dt_exp"], 1)
            for st in STEPS:
                kind = st[0]
                if kind in ("xt", "ht"):
                    _, i, h = st
                    t0, n = TOK[i]
                    wait_filled(act, st)
                    if st == ("ht", 0, 0):
                        act.wait_ge(S["fst_done"], 6 * 16)
                    dst = (hT if kind == "xt" else hnT)[:, 4 * h:4 * h + 4, t0:t0 + n]
                    nc.scalar.copy(dst, bank(st, 4 * n).rearrange("p (k n) -> p k n", k=4)).then_inc(
                        S["cp_done" if kind == "xt" else "hnT_done"], 1)
                    act.wait_ge(S["cp_done" if kind == "xt" else "hnT_done"], 2 * i + h + 1)
                    act.sem_inc(emptied[BANK[st][0]], 1)
                elif kind == "params":
                    act.wait_ge(S["mag_in"], 1)
                    ac(cf[:, 3, :], cf[:, 1, :], ACT.Exp).then_inc(S["mag_exp"], 1)
                    act.wait_ge(S["lb_in"], 1)
                    ac(lb[:, 0:2, :], lb[:, 0:2, :], ACT.Exp).then_inc(S["lb_exp"], 1)
                elif kind == "proj":
                    _, u, j = st
                    if u[0] == "f":
                        g = int(u[1])
                        wait_filled(act, st)
                        if g:
                            act.wait_ge(S["kl_done"], g)
                        is_emptied(ac(kk[:, j, :], bank(st, NT), ACT.Sigmoid), st)
                        if j == 3:
                            act.wait_ge(emptied[BANK[st][0]], BANK[st][1] + 1)
                            act.wait_ge(emptied[1 - BANK[st][0]], BANK[("proj", u, 2)][1] + 1)
                            act.sem_inc(S["f_done"], 1)
                    elif u[0] == "v":
                        g, n = int(u[1]), TOK[j][1]
                        wait_filled(act, st)
                        if g and j == 0:
                            act.wait_ge(filled[BANK[("o", 0, GH - 1)][0]], BANK[("o", 0, GH - 1)][1] + 1)
                            act.wait_ge(S["vm_done"], GH)
                        nc.scalar.copy(vn[0:n, j, :], bank(st, 512, n)).then_inc(S["v_done"], 1)
                        act.wait_ge(S["v_done"], 3 * g + j + 1)
                        act.sem_inc(emptied[BANK[st][0]], 1)
                    elif u[0] == "o":
                        h = GH * int(u[1]) + j
                        wait_filled(act, st)
                        if h >= 2:
                            act.wait_ge(S["o_final"], h - 1)
                        ac(sga[:, h % 2, :], bank(st, NT), ACT.Silu).then_inc(S["sil_o"], 1)
                        act.wait_ge(S["sil_o"], h + 1)
                        act.sem_inc(emptied[BANK[st][0]], 1)
                    elif u[0:2] == "ga":
                        m = 4 * int(u[2]) + j
                        wait_filled(act, st)
                        if m == 0:
                            act.wait_ge(S["o_final"], HEADS)
                        if m >= 2:
                            act.wait_ge(S["merged_ok"], m - 1)
                        ac(sga[:, m % 2, :], bank(st, NT), ACT.Sigmoid).then_inc(S["sig_a"], 1)
                        act.wait_ge(S["sig_a"], m + 1)
                        act.sem_inc(emptied[BANK[st][0]], 1)
                    elif u == "zg":
                        wait_filled(act, st)
                        if j == 0:
                            act.wait_ge(S["merged_ok"], KD)
                        if j >= 2:
                            act.wait_ge(S["yb_done"], j - 1)
                        ac(sga[:, j % 2, :], bank(st, NT), ACT.Sigmoid, bias=pcol[:, 32 + j:33 + j]).then_inc(S["sig_g"], 1)
                        act.wait_ge(S["sig_g"], j + 1)
                        act.sem_inc(emptied[BANK[st][0]], 1)
                    elif u[0:2] == "gb":
                        m = 4 * int(u[2]) + j
                        wait_filled(act, st)
                        if m == 0:
                            act.wait_ge(S["yb_done"], KD)
                        if m >= 2:
                            act.wait_ge(S["merged_ok"], KD + 2 * (m - 1))
                        ac(sga[:, m % 2, :], bank(st, NT), ACT.Sigmoid).then_inc(S["yb_sig"], 1)
                        act.wait_ge(S["yb_sig"], m + 1)
                        act.sem_inc(emptied[BANK[st][0]], 1)
                elif kind == "elem":
                    g = st[1]
                    act.wait_ge(S["lb_done"], 1)
                    act.wait_ge(S["f_done"], g + 1)
                    if g:
                        act.wait_ge(filled[7], BANK[("dss", 0, GH - 1, 1)][1] + 1)
                    for h in range(GH):
                        hh = GH * g + h
                        ac(bc[:, h, :], kk[:, h, :], ACT.Ln, bias=lb[:, LBH, hh:hh + 1],
                           scale=lb[:, OML, hh:hh + 1]).then_inc(S["logf"], 1)
                    act.wait_ge(S["scan_done"], GH * (g + 1))
                    ac(eb[:, :, :], bc[:, :, :], ACT.Exp).then_inc(S["exp_done"], 1)
                    ac(kd[:, :, :], bc[:, :, :], ACT.Exp, scale=-1.0).then_inc(S["exp_done"], 1)
                    act.wait_ge(S["diff_done"], g + 1)
                    ac(bc[:, :, :], bc[:, :, :], ACT.Exp).then_inc(S["dexp"], 1)
                elif kind == "kn":
                    _, g, i = st
                    n = TOK[i][1]
                    wait_filled(act, st)
                    if g:
                        act.wait_ge(S["o_final"], GH)
                    nc.scalar.copy(kn[0:n, i, :], bank(st, 512, n)).then_inc(S["kn_done"], 1)
                    act.wait_ge(S["kn_done"], 3 * g + i + 1)
                    act.sem_inc(emptied[BANK[st][0]], 1)
                elif kind == "sc":
                    _, g, i = st
                    wait_filled(act, st)
                    if i < 2:
                        link(nc.scalar.copy(scp[:, i].rearrange("p h t -> p (h t)"), bank(st)))
                    else:
                        link(nc.scalar.copy(scs[:, :, :].rearrange("p h t -> p (h t)"), bank(st, 256, NS_TOK)))
                    act.sem_inc(emptied[BANK[st][0]], 1)
                    act.sem_inc(S["sc_raw"], 1)
                elif kind == "o":
                    _, g, h = st
                    hh = GH * g + h
                    wait_filled(act, st)
                    nc.scalar.copy(oT[:, hh, :], bank(st, NT)).then_inc(S["o_raw"], 1)
                    act.wait_ge(S["o_raw"], hh + 1)
                    act.sem_inc(emptied[BANK[st][0]], 1)
                elif kind == "mean":
                    _, g, h = st
                    hh = GH * g + h
                    wait_filled(act, st)
                    act.wait_ge(S["on_done"], hh) if hh else None
                    link(ac(rstd_o, bank(st, NT), ACT.Ln, scale=1.0 / P, bias=epsc[:, :]))
                    act.sem_inc(emptied[7], 1)
                    ac(rstd_o, rstd_o, ACT.Exp, scale=-0.5).then_inc(S["rstd_done"], 1)
                elif kind == "sy" and st[1] % 4 == 3:
                    T = st[1] // 4
                    act.wait_ge(S["y5_ev"], T + 1)
                    ac(gy[:, T, :], gy[:, T, :], ACT.Gelu_apprx_tanh).then_inc(S["gy_done"], 1)
                elif kind == "states":
                    wait_filled(act, ("fs",))
                    link(nc.scalar.copy(fstage[0:T5, 0:2, :].rearrange("p r s -> p (r s)"), bank(("fs",), 2 * P, T5)))
                    act.sem_inc(emptied[5], 1)
                    for r, key in enumerate(("re_p", "im_p")):
                        act.dma_start(o[key][0, 0].rearrange("(t q) s -> t (q s)", q=2), fstage[0:T5, r, :]).then_inc(
                            S["fst_done"], 16)
                    act.wait_ge(S["fst_done"], 32)
                    wait_filled(act, ("fss",))
                    link(nc.scalar.copy(fstage[:, 0:2, :].rearrange("p r s -> p (r s)"), bank(("fss",), 2 * P)))
                    act.sem_inc(emptied[6], 1)
                    for r, key in enumerate(("re_s", "im_s")):
                        act.dma_start(o[key][0].rearrange("b (t q) s -> (b t) (q s)", q=2), fstage[:, r, :]).then_inc(
                            S["fst_done"], 32)
                elif kind == "mix" and st[1] == 1:
                    i = st[2]
                    n = TOK[i][1]
                    act.wait_ge(S["h2_done"], 4 + i)
                    if i == 0:
                        wait_filled(act, ("mix", 1, 2))
                    rsqrt_mean(ac(hn[0:n, i, :], h2[0:n, i, :], ACT.Square, accum_out=ss[0:n, i:i + 1]),
                               ss[0:n, i:i + 1], D, S["ss2"])
                elif kind == "rank":
                    pass
            act.wait_ge(S["gexp_in"], 1)
            ac(r32[3][:, :, 0, 0:NG], r32[3][:, :, 0, 0:NG], ACT.Exp).then_inc(S["gexp"], 1)
            ac(r1[8], r1[8], ACT.Exp).then_inc(S["gexp"], 1)
            act.sem_inc(S["hidT_done"], 1)
            act.sem_inc(S["y_copied"], 1)
            for h in range(2):
                act.sem_inc(y_stored[h], 16)
            with act.Fori(0, NE // 2) as it:
                for s in GATE_SLOT:
                    act.wait_ge(used[s], it + (USED[s] + 1))
                ac(sil, ps[2][:, :], ACT.Silu).then_inc(S["silu_done"], 1)
                act.wait_ge(S["hidT_ready"], it + 1)
                nc.scalar.copy(hidT[:, :, :], ps[4][:, :].rearrange("p (k s) -> p k s", k=KE)).then_inc(S["hidT_done"], 1)
                for s in DOWN_SLOT:
                    act.wait_ge(used[s], it + (USED[s] + 1))
                for h in range(2):
                    act.wait_ge(y_stored[h], it * 16 + 16)
                    nc.scalar.copy(yrow[:, h, :], ps[6 + h][:, :]).then_inc(S["y_half"], 1)
                act.wait_ge(S["y_half"], it * 2 + 2)
                act.sem_inc(S["y_copied"], 1)
                for h in range(2):
                    act.dma_start(y_dram[bass.ds(it * P, P), 512 * h:512 * (h + 1)], yrow[:, h, :]).then_inc(
                        y_stored[h], 16)
            act.wait_ge(S["slots"], 1)
            n_ov = act.value_load(ovi[0:1, 15:16], min_val=0, max_val=OV)
            with act.If(n_ov > 0):
                for h in range(2):
                    act.wait_ge(y_stored[h], 16 * (NE // 2 + 1))
                with act.Fori(0, n_ov) as j:
                    act.wait_ge(S["ov_g"], j + 1)
                    ac(sil[0:CAP, :], ps[2][0:CAP, :], ACT.Silu).then_inc(S["ov_sil"], 1)
                    act.wait_ge(S["ov_t"], j + 1)
                    nc.scalar.copy(hidT[:, :, 0:CAP], ps[4][:, :].rearrange("p (k s) -> p k s", k=KE)[:, :, 0:CAP]).then_inc(
                        S["ov_hidT"], 1)
                    act.wait_ge(S["ov_dn"], j + 2)
                    for h in range(2):
                        nc.scalar.copy(yrow[0:CAP, h, :], ps[6 + h][0:CAP, :]).then_inc(S["ov_y"], 1)
                    act.wait_ge(S["ov_y"], j * 2 + 2)
                    act.dma_start(y_dram[bass.ds(j * CAP + NE * CAP, CAP), :].rearrange("p (h d) -> p h d", h=2),
                                  yrow[0:CAP, :, :]).then_inc(S["ov_st"], 16)
                    act.wait_ge(S["ov_st"], j * 16 + 16)
            for i, (t0, n) in enumerate(TOK):
                act.wait_ge(S["fin_ss"], i + 1)
                rsqrt_mean(ac(hn[0:n, i, :], h2[0:n, i, :], ACT.Square, accum_out=ss[0:n, i:i + 1]),
                           ss[0:n, i:i + 1], D, S["ss2"])

        @block.gpsimd
        def _(pool):
            gp = nc.gpsimd
            cnt = [0]

            def link(ins):
                cnt[0] += 1
                ins.then_inc(S["pool"], 1)
                pool.wait_ge(S["pool"], cnt[0])

            gp.memset(epsc[:, :], EPS)
            link(gp.memset(zrow, 0.0))
            link(gp.memset(ident[:, :], 0.0))
            link(gp.affine_select(out=ident[:, :], in_=ident[:, :], compare_op=ALU.not_equal, fill=1.0, base=0,
                                  pattern=[[-1, P]], channel_multiplier=1))
            pool.sem_inc(S["consts"], 1)
            pool.dma_start(y_dram[NE * CAP:, :].rearrange("(j p) d -> p j d", p=CAP),
                           zrow[:, :].unsqueeze(1).broadcast_to([CAP, OV, D])).then_inc(S["zeroed"], 16)
            link(gp.memset(ones[:, :], 1.0))
            link(gp.affine_select(out=upper[:, :], in_=ones[:, :], compare_op=ALU.is_gt, fill=0.0, base=0,
                                  pattern=[[1, P]], channel_multiplier=-1))
            gp.memset(cmask[:, :], 1.0)
            link(gp.memset(smask[:, :], 1.0))
            for c in range(NCH):
                gp.memset(cmask[:, CH * c:CH * c + 1], 0.0)
            gp.memset(smask[:, 0:1], 0.0)
            gp.memset(cmask[:, NP_TOK:NT:SEQ_S], 0.0)
            link(gp.memset(smask[:, NP_TOK:NT:SEQ_S], 0.0))
            link(gp.memset(seqm[:, :], 1.0))
            link(gp.affine_select(out=seqm[:, :], in_=seqm[:, :], compare_op=ALU.is_ge, fill=0.0, base=0,
                                  pattern=[[-SEQ_S, NB]], channel_multiplier=1))
            link(gp.affine_select(out=seqm[:, :], in_=seqm[:, :], compare_op=ALU.is_ge, fill=0.0, base=SEQ_S - 1,
                                  pattern=[[SEQ_S, NB]], channel_multiplier=-1))
            gp.iota(par_i[:, 0:1], pattern=[[0, 1]], base=0, channel_multiplier=1)
            link(gp.iota(iota_i[:, :], pattern=[[1, P]], base=0, channel_multiplier=0))
            link(gp.tensor_copy(iota_s[:, :], iota_i[:, :]))
            link(gp.iota(iota_i[:, 0:NE], pattern=[[-1, NE]], base=NE, channel_multiplier=0))
            link(gp.tensor_copy(rev[:, :], iota_i[:, 0:NE]))
            link(gp.memset(bd[:, :, :, :, :].rearrange("p r t q c -> p (r t q c)"), 0.0))
            pool.sem_inc(S["consts"], 1)

            def tables(half):
                t0 = T5H * half
                if half == 0:
                    pool.wait_ge(S["phasor"], 1)
                    pool.wait_ge(S["zeroed"], 16)
                else:
                    pool.wait_ge(S["g_done"], 2 * T5H)
                link(gp.memset(cosT[:, :, 0:1], 1.0))
                link(gp.memset(sinT[:, :, 0:1], 0.0))
                n = 1
                while n < NP_TOK:
                    L = min(n, P)
                    pc, ps_ = cf[:, 18, t0:t0 + T5H], cf[:, 19, t0:t0 + T5H]
                    if n == 1:
                        gp.tensor_copy(pc, cf[:, 5, t0:t0 + T5H])
                        link(gp.tensor_copy(ps_, cf[:, 6, t0:t0 + T5H]))
                    else:
                        link(gp.tensor_tensor(cf[:, 20, t0:t0 + T5H], pc, pc, ALU.mult))
                        link(gp.tensor_tensor(cf[:, 21, t0:t0 + T5H], ps_, ps_, ALU.mult))
                        link(gp.tensor_tensor(cf[:, 22, t0:t0 + T5H], pc, ps_, ALU.mult))
                        link(gp.tensor_tensor(pc, cf[:, 20, t0:t0 + T5H], cf[:, 21, t0:t0 + T5H], ALU.subtract))
                        link(gp.tensor_tensor(ps_, cf[:, 22, t0:t0 + T5H], cf[:, 22, t0:t0 + T5H], ALU.add))
                    tv = ptab[:, 0:T5H * n].rearrange("p (t n) -> p t n", t=T5H) if n < P else \
                        ptab.rearrange("p (t n) -> p t n", t=T5H)
                    link(gp.tensor_tensor(cosT[:, :, n:2 * n], cosT[:, :, 0:n], bt(pc, n), ALU.mult))
                    link(gp.tensor_tensor(tv, sinT[:, :, 0:n], bt(ps_, n), ALU.mult))
                    link(gp.tensor_tensor(cosT[:, :, n:2 * n], cosT[:, :, n:2 * n], tv, ALU.subtract))
                    link(gp.tensor_tensor(sinT[:, :, n:2 * n], sinT[:, :, 0:n], bt(pc, n), ALU.mult))
                    link(gp.tensor_tensor(tv, cosT[:, :, 0:n], bt(ps_, n), ALU.mult))
                    link(gp.tensor_tensor(sinT[:, :, n:2 * n], sinT[:, :, n:2 * n], tv, ALU.add))
                    n *= 2
                for T in (cosT, sinT):
                    for b in range(NB):
                        last = gp.tensor_copy(T[:, :, NP_TOK + SEQ_S * b:NP_TOK + SEQ_S * (b + 1)], T[:, :, 0:SEQ_S])
                    link(last)
                pool.sem_inc(S["tab_done"], 1)

            tables(0)
            for st in STEPS:
                kind = st[0]
                if kind == "elem":
                    g = st[1]
                    pool.wait_ge(S["exp_done"], 2 * g + 1)
                    pool.wait_ge(S["q_done"], GH * (g + 1))
                    if g:
                        key = ("o", 0, GH - 1)
                        pool.wait_ge(filled[BANK[key][0]], BANK[key][1] + 1)
                    gp.tensor_tensor(qd[:, :, :], oT[:, GH:, :] if g else qd[:, :, :], eb[:, :, :], ALU.mult).then_inc(S["qd_done"], 1)
                    pool.wait_ge(S["qd_done"], g + 1)
                    pool.wait_ge(S["exp_done"], 2 * g + 2)
                    pool.wait_ge(S["k_done"], GH * (g + 1))
                    gp.tensor_tensor(kd[:, :, :], kd[:, :, :], kk[:, :, :], ALU.mult).then_inc(S["kd_done"], 1)
                    pool.wait_ge(S["kd_done"], g + 1)
                    pool.wait_ge(S["dexp"], g + 1)
                    gp.tensor_tensor(bc[:, :, :], bc[:, :, :], kk[:, :, :], ALU.mult).then_inc(S["kl_done"], 1)
                    pool.wait_ge(S["kl_done"], g + 1)
                elif kind == "sc":
                    _, g, i = st
                    pool.wait_ge(S["sc_raw"], 3 * g + i + 1)
                    if i < 2:
                        link(gp.affine_select(out=scp[:, i], in_=scp[:, i], compare_op=ALU.is_ge, fill=0.0, base=0,
                                              pattern=[[0, GH], [1, P]], channel_multiplier=-1))
                        link(gp.memset(scp[0:CH, i, :, CH:P], 0.0))
                        pool.sem_inc(S["sc_done"], 1)
                    else:
                        link(gp.affine_select(out=scs[:, :, :], in_=scs[:, :, :], compare_op=ALU.is_ge, fill=0.0, base=0,
                                              pattern=[[0, GH], [1, NS_TOK]], channel_multiplier=-1))
                        v = scs[:, :, :].rearrange("p h (b s) -> p h b s", s=SEQ_S)
                        link(gp.affine_select(out=v, in_=v, compare_op=ALU.is_ge, fill=0.0, base=0,
                                              pattern=[[0, GH], [-SEQ_S, NB], [0, SEQ_S]], channel_multiplier=1))
                        pool.sem_inc(S["sc_done"], 1)
                elif kind == "o":
                    _, g, h = st
                    hh = GH * g + h
                    pool.wait_ge(filled[BANK[st][0]], BANK[st][1] + 1)
                    pool.wait_ge(st_in[h % 2], 16 * (hh // 2 + 1))
                    pool.wait_ge(S["lb_done"], 1)
                    v = stt_[:, h % 2]
                    gp.tensor_tensor(v, v, bt(eblast[:, h, NCH:], P), ALU.mult).then_inc(S["st_scaled"], 1)
                    pool.wait_ge(S["st_scaled"], hh + 1)
                elif kind == "mean":
                    _, g, h = st
                    hh = GH * g + h
                    pool.wait_ge(S["o_raw"], hh + 1)
                    if hh:
                        pool.wait_ge(filled[7], BANK[("mean", (hh - 1) // GH, (hh - 1) % GH)][1] + 1)
                    gp.tensor_tensor(osq, oT[:, hh, :], oT[:, hh, :], ALU.mult).then_inc(S["sq_done"], 1)
                    pool.wait_ge(S["sq_done"], hh + 1)
                elif kind == "bu":
                    t = st[1]
                    s, tt = t % 2, t % T5H
                    pool.wait_ge(S["g_done"], 2 * t + 2)
                    if t >= 2:
                        pool.wait_ge(S["h_used"], t - 1)
                        pool.wait_ge(S["fs_done"], t - 1)
                    C, Sn = cosT[:, tt, :], sinT[:, tt, :]
                    link(gp.tensor_tensor(pt1, gr[:, s, :], C, ALU.mult))
                    link(gp.tensor_tensor(pt2, gi[:, s, :], Sn, ALU.mult))
                    link(gp.tensor_tensor(hr[:, s, :], pt1, pt2, ALU.subtract))
                    link(gp.tensor_tensor(pt1, gr[:, s, :], Sn, ALU.mult))
                    link(gp.tensor_tensor(pt2, gi[:, s, :], C, ALU.mult))
                    gp.tensor_tensor(hi[:, s, :], pt1, pt2, ALU.add).then_inc(S["h_done"], 1)
                    pool.wait_ge(S["h_done"], t + 1)
                    if t == T5H - 1:
                        tables(1)
            pool.wait_ge(S["slots"], 1)
            n_ov = pool.value_load(ovi[0:1, 15:16], min_val=0, max_val=OV)
            for e in range(2):
                pool.wait_ge(y_stored[e], 16 * (NE // 2 + 1))
            with pool.If(n_ov > 0):
                pool.wait_ge(S["ov_st"], n_ov * 16)
            for i, (t0, n) in enumerate(TOK):
                if i == 2:
                    pool.wait_ge(S["fin_ss"], 1)
                for k, dst in enumerate((ya, yb)):
                    gp.indirect_dma_start(dst[0:n, i % 2, :], None, y_dram[:, :],
                                          bass.IndirectOffsetOnAxis(ap=sidx[0:n, i, k:k + 1].bitcast(U32), axis=0)).then_inc(
                        gathered[i % 2], 16)

        @block.vector
        def _(dve):
            v_ = nc.vector
            cnt = [0]

            def link(ins):
                cnt[0] += 1
                ins.then_inc(S["dve"], 1)
                dve.wait_ge(S["dve"], cnt[0])

            TT, TS, STT = v_.tensor_tensor, v_.tensor_scalar, v_.scalar_tensor_tensor
            dve.wait_ge(gmix_in, 16)
            for i, (t0, n) in enumerate(TOK):
                dve.wait_ge(S["ss_done"], i + 1)
                if i == 2:
                    dve.wait_ge(filled[BANK[("xt", 0, 1)][0]], BANK[("xt", 0, 1)][1] + 1)
                STT(xn[0:n, i % 2, :], h2[0:n, i, :], ss[0:n, i:i + 1], grow[0:n, :], ALU.mult, ALU.mult).then_inc(
                    S["xn_done"], 1)
            C = lambda i: cf[:, i, :]
            lre, lim = pcol[:, 44:60], pcol[:, 60:76]

            def params():
                st = ("params",)
                wait_filled(dve, st)
                is_emptied(v_.tensor_copy(pcol[:, :], bank(st, 76)), st)
                dve.wait_ge(emptied[BANK[st][0]], BANK[st][1] + 1)
                dve.wait_ge(S["dt_exp"], 2)
                link(TT(C(1), lre, C(0), ALU.mult))
                dve.sem_inc(S["mag_in"], 1)
                r0, r1_ = pcol[:, 0:8], pcol[:, 8:16]
                link(TT(lb[:, 2, :], r0, r1_, ALU.max))
                TT(lb[:, 0, :], r0, lb[:, 2, :], ALU.subtract)
                link(TT(lb[:, 1, :], r1_, lb[:, 2, :], ALU.subtract))
                dve.sem_inc(S["lb_in"], 1)
                link(TT(C(2), lim, C(0), ALU.mult))
                link(TS(C(4), C(2), 1.0 / (2 * np.pi), 12582912.0, ALU.mult, ALU.add))
                link(TS(C(4), C(4), -12582912.0, None, ALU.add))
                two_pi = 2 * np.pi
                c1 = 6.28125
                c2 = float(np.float32(np.floor((two_pi - c1) * 2 ** 21) / 2 ** 21))
                c3 = two_pi - c1 - c2
                for c in (c1, c2, c3):
                    link(STT(C(2), C(4), -c, C(2), ALU.mult, ALU.add))
                link(TS(C(2), C(2), 0.25, None, ALU.mult))
                link(TT(C(7), C(2), C(2), ALU.mult))
                link(TS(C(8), C(7), 1.0 / 362880, -1.0 / 5040, ALU.mult, ALU.add))
                for c in (1.0 / 120, -1.0 / 6, 1.0):
                    link(TT(C(8), C(8), C(7), ALU.mult))
                    link(TS(C(8), C(8), c, None, ALU.add))
                link(TT(C(6), C(8), C(2), ALU.mult))
                link(TS(C(8), C(7), -1.0 / 3628800, 1.0 / 40320, ALU.mult, ALU.add))
                for c in (-1.0 / 720, 1.0 / 24, -0.5, 1.0):
                    link(TT(C(8), C(8), C(7), ALU.mult))
                    link(TS(C(8), C(8), c, None, ALU.add))
                link(v_.tensor_copy(C(5), C(8)))
                for _ in range(2):
                    link(TT(C(8), C(5), C(6), ALU.mult))
                    link(TT(C(9), C(6), C(6), ALU.mult))
                    link(TS(C(6), C(8), 2.0, None, ALU.mult))
                    link(TS(C(5), C(9), -2.0, 1.0, ALU.mult, ALU.add))
                dve.sem_inc(S["phasor"], 1)
                dve.wait_ge(S["mag_exp"], 1)
                TT(C(10), C(3), C(5), ALU.mult)
                TT(C(11), C(3), C(6), ALU.mult)
                link(TT(C(12), lre, lre, ALU.mult))
                link(TT(C(13), lim, lim, ALU.mult))
                link(TT(C(12), C(12), C(13), ALU.add))
                link(v_.reciprocal(C(12), C(12)))
                link(TS(C(13), C(10), -1.0, None, ALU.add))
                TT(C(14), C(13), lre, ALU.mult)
                link(TT(C(15), C(11), lim, ALU.mult))
                link(TT(C(14), C(14), C(15), ALU.add))
                TT(C(15), C(11), lre, ALU.mult)
                link(TT(C(13), C(13), lim, ALU.mult))
                link(TT(C(15), C(15), C(13), ALU.subtract))
                TT(C(14), C(14), C(12), ALU.mult)
                link(TT(C(15), C(15), C(12), ALU.mult))
                dve.wait_ge(S["consts"], 2)
                cr, ci = bt(C(14), CG), bt(C(15), CG)
                for r in range(2):
                    TT(ptmp, braw[:, r], cr, ALU.mult)
                    link(TT(ptmp2, braw[:, 1 - r], ci, ALU.mult))
                    for q in range(2):
                        h = slice(ST * q, ST * (q + 1))
                        last = TT(bd[h, r, :, q, :], ptmp[h], ptmp2[h], ALU.add if r else ALU.subtract)
                    link(last)
                    dve.sem_inc(S["bdcd"], 1)
                link(TS(par_i[:, 1:2], par_i[:, 0:1], 4, 1, ALU.logical_shift_right, ALU.bitwise_and))
                link(v_.tensor_copy(par[:, 1:2], par_i[:, 1:2]))
                link(TS(par[:, 0:1], par[:, 1:2], -1.0, 1.0, ALU.mult, ALU.add))
                link(TS(negp[:, :], par[:, :], -1.0, None, ALU.mult))
                for r in range(2):
                    for q in range(2):
                        last = TS(cd[:, r, :, q, :], craw[:, r], (negp if r else par)[:, q:q + 1], None, ALU.mult)
                    link(last)
                    dve.sem_inc(S["bdcd"], 1)
                dve.wait_ge(S["lb_exp"], 1)
                link(TT(lb[:, 2, :], lb[:, 0, :], lb[:, 1, :], ALU.add))
                link(v_.reciprocal(lb[:, 2, :], lb[:, 2, :]))
                link(TT(lb[:, 0, :], lb[:, 0, :], lb[:, 2, :], ALU.mult))
                link(TS(lb[:, OML, :], lb[:, 0, :], -1.0, 1.0, ALU.mult, ALU.add))
                link(TS(lb[:, NOML, :], lb[:, OML, :], -1.0, None, ALU.mult))
                dve.sem_inc(S["lb_done"], 1)

            heads_done = [0]
            for st in STEPS:
                kind = st[0]
                if kind == "params":
                    params()
                elif kind == "h0":
                    wait_filled(dve, st)
                    is_emptied(v_.tensor_copy(arena[:, int(113.5 * K):int(113.5 * K) + 2 * P], bank(st, 2 * P)), st)
                    dve.wait_ge(emptied[BANK[st][0]], BANK[st][1] + 1)
                    for r in range(2):
                        hv = ptmp.rearrange("p t c -> p (t c)")[:, 0:P].rearrange("p (t b) -> p t b", b=NB)
                        TT(ah[:, r], h0t[:, r], bt(C(10), NB), ALU.mult)
                        link(TT(hv, h0t[:, 1 - r], bt(C(11), NB), ALU.mult))
                        link(TT(ah[:, r], ah[:, r], hv, ALU.add if r else ALU.subtract))
                elif kind in ("bt", "ct"):
                    wait_filled(dve, st)
                    dst = (btr if kind == "bt" else ctr)[:, st[1]].rearrange("p t n -> p (t n)")
                    link(v_.tensor_copy(dst, bank(st)))
                    dve.sem_inc(emptied[BANK[st][0]], 1)
                    dve.sem_inc(S["bdcd"], 1)
                elif kind == "proj":
                    _, u, j = st
                    if u == "u":
                        wait_filled(dve, st)
                        v_.tensor_copy(uT[:, j, :], bank(st, NT)).then_inc(S["u_done"], 1)
                        dve.wait_ge(S["u_done"], j + 1)
                        dve.sem_inc(emptied[BANK[st][0]], 1)
                    elif u[0] == "q":
                        g = int(u[1])
                        wait_filled(dve, st)
                        TS(oT[:, GH + j, :] if g else qd[:, j, :], bank(st, NT), HG_SCALE, None, ALU.mult).then_inc(S["q_done"], 1)
                        dve.wait_ge(S["q_done"], GH * g + j + 1)
                        dve.sem_inc(emptied[BANK[st][0]], 1)
                    elif u[0] == "o":
                        hh = GH * int(u[1]) + j
                        dve.wait_ge(S["sil_o"], hh + 1)
                        dve.wait_ge(S["on_done"], hh + 1)
                        STT(oT[:, hh, :], oT[:, hh, :], pcol[:, 16 + hh:17 + hh], sga[:, hh % 2, :], ALU.mult,
                            ALU.mult).then_inc(S["o_final"], 1)
                    elif u[0:2] == "wa":
                        pass
                    elif u[0:2] == "ga":
                        m = 4 * int(u[2]) + j
                        wa = ("proj", f"wa{u[2]}", j)
                        wait_filled(dve, wa)
                        dve.wait_ge(S["sig_a"], m + 1)
                        TT(merged[:, m, :], bank(wa, NT), sga[:, m % 2, :], ALU.mult).then_inc(S["merged_ok"], 1)
                        dve.wait_ge(S["merged_ok"], m + 1)
                        dve.sem_inc(emptied[BANK[wa][0]], 1)
                    elif u == "zg":
                        za = ("proj", "za", j)
                        wait_filled(dve, za)
                        dve.wait_ge(S["sig_g"], j + 1)
                        STT(oT[:, j, :], bank(za, NT), pcol[:, 24 + j:25 + j], sga[:, j % 2, :], ALU.add,
                            ALU.mult).then_inc(S["yb_done"], 1)
                        dve.wait_ge(S["yb_done"], j + 1)
                        dve.sem_inc(emptied[BANK[za][0]], 1)
                    elif u[0:2] == "gb":
                        m = 4 * int(u[2]) + j
                        dve.wait_ge(S["yb_sig"], m + 1)
                        TT(oT[:, m, :], oT[:, m, :], sga[:, m % 2, :], ALU.mult).then_inc(S["merged_ok"], 1)
                        dve.wait_ge(S["merged_ok"], KD + 2 * m + 1)
                        TT(merged[:, m, :], merged[:, m, :], oT[:, m, :], ALU.add).then_inc(S["merged_ok"], 1)
                elif kind == "elem":
                    g = st[1]
                    dve.wait_ge(S["logf"], GH * (g + 1))
                    for h in range(GH):
                        hh = GH * g + h
                        TS(kk[:, h, :], kk[:, h, :], lb[:, NOML, hh:hh + 1], lb[:, OML, hh:hh + 1], ALU.mult,
                           ALU.add).then_inc(S["k_done"], 1)
                    for h in range(GH):
                        v_.tensor_tensor_scan(bc[:, h, :], cmask[:, :], bc[:, h, :], 0.0, ALU.mult, ALU.add).then_inc(
                            S["scan_done"], 1)
                    dve.wait_ge(S["exp_done"], 2 * g + 2)
                    v_.tensor_copy(blast[:, :, 0:NCH], bc[:, :, CH - 1:NP_TOK:CH])
                    v_.tensor_copy(blast[:, :, NCH:], bc[:, :, NP_TOK + SEQ_S - 1:NT:SEQ_S])
                    v_.tensor_copy(eblast[:, :, 0:NCH], eb[:, :, CH - 1:NP_TOK:CH])
                    link(v_.tensor_copy(eblast[:, :, NCH:], eb[:, :, NP_TOK + SEQ_S - 1:NT:SEQ_S]))
                    for h in range(GH):
                        for (c0, c1, n, lo) in ((0, NCH, CH, 0), (NCH, 12, SEQ_S, NP_TOK)):
                            v = bc[:, h, lo:lo + (c1 - c0) * n].rearrange("p (c s) -> p c s", s=n)
                            last = TT(v, bt(blast[:, h, c0:c1], n), v, ALU.subtract)
                    last.then_inc(S["diff_done"], 1)
                elif kind == "ds":
                    _, g, c = st
                    wait_filled(dve, st)
                    if g and c == 0:
                        dve.wait_ge(S["out_done"], 16)
                        dve.wait_ge(filled[BANK[("o", 0, GH - 1)][0]], BANK[("o", 0, GH - 1)][1] + 1)
                    for h in range(GH):
                        cs = slice(h * P, (h + 1) * P)
                        if c == 0:
                            last = v_.tensor_copy(sp_[:, 0, cs], ps[7][:, cs])
                        else:
                            last = STT(sp_[:, c, cs], sp_[:, c - 1, cs], eblast[:, h, c:c + 1], ps[7][:, cs], ALU.mult,
                                       ALU.add)
                    last.then_inc(S["state_new"], 1)
                    dve.wait_ge(S["state_new"], NCH * g + c + 1)
                    dve.sem_inc(emptied[7], 1)
                elif kind == "o":
                    _, g, h = st
                    hh = GH * g + h
                    dve.wait_ge(S["v_done"], 3 * (g + 1))
                    if hh:
                        key = ("dss", (hh - 1) // GH, (hh - 1) % GH, 1)
                        dve.wait_ge(filled[7], BANK[key][1] + 1)
                    TT(vm[:, :, :], vn[0:NS_TOK, 2, h * P:(h + 1) * P].unsqueeze(1).broadcast_to([NS_TOK, NB, P]),
                       bt(seqm[:, :], P), ALU.mult).then_inc(S["vm_done"], 1)
                elif kind == "dss":
                    _, g, h, i = st
                    hh = GH * g + h
                    wait_filled(dve, st)
                    dve.wait_ge(S["st_scaled"], hh + 1)
                    v = stt_[:, h % 2, 4 * i:4 * i + 4, :].rearrange("p b v -> p (b v)")
                    TT(v, bank(st), v, ALU.add).then_inc(S["st_sum"], 1)
                    dve.wait_ge(S["st_sum"], 2 * hh + i + 1)
                    dve.sem_inc(emptied[7], 1)
                elif kind == "mean":
                    _, g, h = st
                    hh = GH * g + h
                    dve.wait_ge(S["rstd_done"], hh + 1)
                    TT(oT[:, hh, :], oT[:, hh, :], rstd_o, ALU.mult).then_inc(S["on_done"], 1)
                elif kind == "bu":
                    t = st[1]
                    s, tt = t % 2, t % T5H
                    if tt == 0:
                        dve.wait_ge(S["tab_done"], t // T5H + 1)
                    Ct, Sn = cosT[:, tt, :], sinT[:, tt, :]
                    wait_filled(dve, ("bur", t))
                    wait_filled(dve, ("bui", t))
                    br, bi = bank(("bur", t), NT), bank(("bui", t), NT)
                    if t:
                        dve.wait_ge(S["g_done"], 2 * t)
                    TT(wr, br, Ct, ALU.mult)
                    TT(tm1, bi, Sn, ALU.mult)
                    TT(wi, bi, Ct, ALU.mult)
                    link(TT(tm2, br, Sn, ALU.mult))
                    dve.sem_inc(emptied[2], 1)
                    dve.sem_inc(emptied[3], 1)
                    TT(wr, wr, tm1, ALU.add)
                    TT(wi, wi, tm2, ALU.subtract)
                    link(TS(rdec, smask[:, :], cf[:, 3, t:t + 1], None, ALU.mult))
                    TT(wr[:, NP_TOK:NT:SEQ_S], wr[:, NP_TOK:NT:SEQ_S], ah[:, 0, t, :], ALU.add)
                    link(TT(wi[:, NP_TOK:NT:SEQ_S], wi[:, NP_TOK:NT:SEQ_S], ah[:, 1, t, :], ALU.add))
                    if t >= 2:
                        dve.wait_ge(S["h_done"], t - 1)
                    v_.tensor_tensor_scan(gr[:, s, :], rdec, wr, 0.0, ALU.mult, ALU.add).then_inc(S["g_done"], 1)
                    v_.tensor_tensor_scan(gi[:, s, :], rdec, wi, 0.0, ALU.mult, ALU.add).then_inc(S["g_done"], 1)
                elif kind == "sy":
                    t = st[1]
                    s = t % 2
                    dve.wait_ge(S["h_done"], t + 1)
                    for r, hv in enumerate((hr, hi)):
                        v_.tensor_copy(fsp[:, r, t:t + 1], hv[:, s, NP_TOK - 1:NP_TOK])
                        last = v_.tensor_copy(fss[:, r, :, t], hv[:, s, NP_TOK + SEQ_S - 1:NT:SEQ_S])
                    last.then_inc(S["fs_done"], 1)
                    if t % 4 == 3:
                        T = t // 4
                        dve.wait_ge(S["h_used"], t + 1)
                        STT(gy[:, T, :], uT[:, T, :], pcol[:, 40 + T:41 + T], ps[4][:, 0:NT], ALU.mult, ALU.add).then_inc(
                            S["y5_ev"], 1)
                        dve.wait_ge(S["y5_ev"], T + 1)
                        dve.sem_inc(emptied[4], 1)
                elif kind == "mix":
                    _, h, i = st
                    n = TOK[i][1]
                    wait_filled(dve, st)
                    hv = h2[0:n, i, 512 * h:512 * (h + 1)]
                    TT(hv, bank(st, 512, n), hv, ALU.add).then_inc(S["h2_done"], 1)
                    dve.wait_ge(S["h2_done"], 3 * h + i + 1)
                    dve.sem_inc(emptied[BANK[st][0]], 1)
                    if h == 1:
                        dve.wait_ge(late_in, 9 * 16)
                        dve.wait_ge(S["ss2"], i + 1)
                        by_p = lambda v: v.rearrange("p (c k) -> p c k", k=KD)
                        STT(hn[0:n, i, :].rearrange("p (k c) -> p c k", k=KD), by_p(h2[0:n, i, :]), ss[0:n, i:i + 1],
                            by_p(gffn[0:n, :]), ALU.mult, ALU.mult).then_inc(
                            S["hn_done"], 1)
                elif kind == "logits":
                    i = st[1]
                    n = TOK[i][1]
                    if i == 0:
                        link(v_.memset(lg[:, :, :], 0.0))
                    wait_filled(dve, st)
                    link(TT(lg[0:n, i, :], bank(st, NG + NE, n), brt[0:n, :], ALU.add))
                    dve.sem_inc(emptied[BANK[st][0]], 1)
                elif kind == "rank":
                    break

            RED = v_.tensor_reduce
            gl = lg[:, :, 0:NG]
            el = lg[:, :, NG:].rearrange("p t (g e) -> p t g e", g=NG)
            A1, A2, M = r32[0], r32[1], r32[2]
            rv4 = rev[:, NE - NG:].unsqueeze(1).broadcast_to([P, 3, NG])
            rv8 = rev[:, NE - NE_G:].unsqueeze(1).broadcast_to([P, 3, NE_G])
            gx = r32[3][:, :, 0, 0:NG]
            link(RED(r1[0], gl, X, ALU.max))
            link(TT(gx, gl, r1[0].broadcast_to([P, 3, NG]), ALU.subtract))
            e4 = r8[0][:, :, 0:NG]
            og = r8[1][:, :, 0:NG]
            link(TS(e4, gx, 0.0, None, ALU.is_equal))
            link(TT(e4, e4, rv4, ALU.mult))
            link(RED(r1[1], e4, X, ALU.max))
            link(TT(og, rv4, r1[1].broadcast_to([P, 3, NG]), ALU.is_equal))
            link(TT(r32[4], el, bt(og, NE_G), ALU.mult))
            es = r8[2]
            link(RED(es, r32[4].rearrange("p t g e -> p t e g"), X, ALU.add))
            oh = []
            for k in range(2):
                vmax = r1[2 + k]
                link(RED(vmax, es, X, ALU.max))
                link(TT(r8[3], es, vmax.broadcast_to([P, 3, NE_G]), ALU.is_equal))
                link(TT(r8[3], r8[3], rv8, ALU.mult))
                link(RED(r1[4], r8[3], X, ALU.max))
                link(TT(r8[4 + k], rv8, r1[4].broadcast_to([P, 3, NE_G]), ALU.is_equal))
                oh.append(r8[4 + k])
                if k == 0:
                    link(STT(es, r8[4], -BIG, es, ALU.mult, ALU.add))
            link(TT(r1[8], r1[3], r1[2], ALU.subtract))
            for k, A in enumerate((A1, A2)):
                link(TT(A, bt(og, NE_G), oh[k].unsqueeze(2).broadcast_to([P, 3, NG, NE_G]), ALU.mult))
                link(v_.memset(A[NS_TOK:P, 2, :, :], 0.0))
            link(TT(M, A1, A2, ALU.add))
            dve.sem_inc(S["mats"], 1)
            dve.sem_inc(S["gexp_in"], 1)
            dve.wait_ge(S["gexp"], 2)
            link(RED(r1[5], gx, X, ALU.add))
            link(TS(r1[6], r1[8], 1.0, None, ALU.add))
            link(TT(r1[5], r1[5], r1[6], ALU.mult))
            link(v_.reciprocal(r1[5], r1[5]))
            link(v_.tensor_copy(wtop[:, 0, :].unsqueeze(2), r1[5]))
            link(TT(wtop[:, 1, :].unsqueeze(2), r1[5], r1[8], ALU.mult))
            st = ("rank",)
            wait_filled(dve, st)
            rk = r32[5]
            link(v_.tensor_copy(rk.rearrange("p t g e -> p (t g e)"), bank(st, 3 * NE)))
            link(v_.tensor_copy(nE, ps[BANK[st][0]][:, 3 * NE:4 * NE]))
            dve.sem_inc(emptied[BANK[st][0]], 1)
            link(TS(ovt, nE, float(CAP), None, ALU.is_gt))
            for k in range(2, (NT + CAP - 1) // CAP):
                link(STT(ovt, nE, float(CAP * k), ovt, ALU.is_gt, ALU.add))
            link(v_.tensor_tensor_scan(incl, ones[:, 0:NE], ovt, 0.0, ALU.mult, ALU.add))
            link(TT(corr, incl, ovt, ALU.subtract))
            link(TT(corr, corr, rev[:, :], ALU.add))
            link(TS(corr, corr, -1.0, float(CAP), ALU.add, ALU.mult))
            flat = lambda v: v.rearrange("p t g e -> p t (g e)")
            b3 = lambda v: v.unsqueeze(1).broadcast_to([P, 3, NE])
            link(TS(r32[6], rk, float(CAP), None, ALU.is_ge))
            link(TT(flat(r32[6]), flat(r32[6]), b3(corr), ALU.mult))
            link(TT(r32[6], r32[6], rk, ALU.add))
            link(TS(r32[7].rearrange("p t g e -> p (t g e)")[:, 0:NE], iota_s[:, 0:NE], float(CAP), None,
                                  ALU.mult))
            link(TT(flat(r32[6]), flat(r32[6]), b3(r32[7].rearrange("p t g e -> p (t g e)")[:, 0:NE]), ALU.add))
            for k, A in enumerate((A1, A2)):
                link(TT(r32[3], A, r32[6], ALU.mult))
                link(RED(slot[:, k, :].unsqueeze(2), flat(r32[3]), X, ALU.add))
                link(v_.tensor_copy(sidx[:, :, k], slot[:, k, :]))
                link(v_.memset(slot[NS_TOK:P, k, 2:3], -1.0e9))
            link(TT(ovj, incl.unsqueeze(1).broadcast_to([P, OV, NE]), bt(iota_s[:, 0:OV], NE), ALU.is_le))
            link(RED(r8[6].rearrange("p t e -> p (t e)")[:, 0:OV].unsqueeze(2), ovj, X, ALU.add))
            link(TS(r8[6].rearrange("p t e -> p (t e)")[:, 0:OV], r8[6].rearrange("p t e -> p (t e)")[:, 0:OV],
                    float(NE - 1), None, ALU.min))
            link(v_.tensor_copy(ovi[:, 0:OV], r8[6].rearrange("p t e -> p (t e)")[:, 0:OV]))
            link(v_.tensor_copy(ovi[:, 15:16], incl[:, NE - 1:NE]))
            dve.sem_inc(S["slots"], 1)

            def build(width, first, shifted, done, picked):
                for i in range(3):
                    last = TS(pick[:, i, 0:width], iota_s[:, 0:width], slot[:, 0, i:i + 1], None, ALU.is_equal)
                last.then_inc(S["dve"], 1)
                dve.wait_ge(S["dve"], first)
                for i in range(3):
                    last = STT(pick[:, i, 0:width], iota_s[:, 0:width], slot[:, 1, i:i + 1], pick[:, i, 0:width],
                               ALU.is_equal, ALU.add)
                last.then_inc(S[done], 1)
                dve.wait_ge(S[done], picked)
                TS(slot[:, :, :], slot[:, :, :], -float(width), None, ALU.add).then_inc(S["dve"], 1)
                dve.wait_ge(S["dve"], shifted)

            def copy_xT(width):
                for b in range(2):
                    last = v_.tensor_copy(xT[:, 4 * b:4 * b + 4, 0:width],
                                          ps[b][:, :].rearrange("p (k s) -> p k s", k=4)[:, :, 0:width])
                return last

            for n in range(2):
                if n:
                    dve.wait_ge(S["sel_done"], 1)
                    copy_xT(P).then_inc(S["xT_done"], 1)
                build(P, cnt[0] + 1, cnt[0] + 2, "pick_done", n + 1)
                cnt[0] += 2
            dve.sem_inc(S["hid_done"], 1)
            b0 = cnt[0]
            with dve.Fori(0, NE // 2) as it:
                for s in UP_SLOT:
                    dve.wait_ge(used[s], it + (USED[s] + 1))
                dve.wait_ge(S["silu_done"], it + 1)
                in_order = lambda v, rows: v[0:rows, :].rearrange("p (c k) -> p k c", k=KE)
                TT(hid[:, :].rearrange("p (k c) -> p k c", k=KE), in_order(ps[3], P), in_order(sil, P),
                   ALU.mult).then_inc(S["hid_done"], 1)
                dve.wait_ge(S["sel_done"], it + 2)
                copy_xT(P).then_inc(S["xT_done"], 1)
                build(P, it * 2 + (b0 + 1), it * 2 + (b0 + 2), "pick_done", it + 3)
            b1 = b0 + NE
            link_val = b1 + 1
            TS(slot[:, :, :], slot[:, :, :], 2.0 * P, None, ALU.add).then_inc(S["dve"], 1)
            dve.wait_ge(S["dve"], link_val)
            n_ov = dve.value_load(ovi[0:1, 15:16], min_val=0, max_val=OV)
            with dve.If(n_ov > 0):
                dve.wait_ge(S["sel_done"], NE // 2 + 1)
                with dve.Fori(0, n_ov) as j:
                    build(CAP, j * 2 + (link_val + 1), j * 2 + (link_val + 2), "ov_p", j + 1)
                    dve.wait_ge(S["ov_sel"], j + 1)
                    copy_xT(CAP).then_inc(S["ov_x"], 1)
                    dve.wait_ge(S["ov_u"], j + 1)
                    dve.wait_ge(S["ov_sil"], j + 1)
                    TT(hid[0:CAP, :].rearrange("p (k c) -> p k c", k=KE), in_order(ps[3], CAP), in_order(sil, CAP),
                       ALU.mult).then_inc(S["ov_hid"], 1)
            fin = S["fin_ss"]
            for i, (t0, n) in enumerate(TOK):
                dve.wait_ge(gathered[i % 2], 32 * (i // 2 + 1))
                hv = h2[0:n, i, :]
                STT(hv, ya[0:n, i % 2, :], wtop[0:n, 0, i:i + 1], hv, ALU.mult, ALU.add).then_inc(S["merged_ok"], 1)
                dve.wait_ge(S["merged_ok"], 3 * KD + i + 1)
                STT(hv, yb[0:n, i % 2, :], wtop[0:n, 1, i:i + 1], hv, ALU.mult, ALU.add).then_inc(fin, 1)
                dve.wait_ge(S["ss2"], 4 + i)
                STT(hv, hv, ss[0:n, i:i + 1], gfin[0:n, :], ALU.mult, ALU.mult).then_inc(S["fin_done"], 1)


_INS = ["x_prompt", "x_sample", "state_hgrn", "state_s5_re", "state_s5_im", "norm_mix_g", "w_in", "hgrn_lb_raw",
        "hgrn_onorm_g", "w_branch_a", "s5_lambda_re", "s5_lambda_im", "s5_log_dt", "s5_b_re", "s5_b_im", "s5_c_re",
        "s5_c_im", "s5_d", "w_glu", "b_glu", "w_out", "norm_ffn_g", "w_router_group", "b_router_group",
        "w_router_expert", "b_router_expert", "w_exp_gate", "w_exp_up", "w_exp_down", "norm_final_g"]
_OUTS = [("y_p", (1, 256, 1024)), ("y_s", (8, 8, 1024)), ("hg_p", (1, 1, 8, 128, 128)), ("re_p", (1, 1, 32, 64)),
         ("im_p", (1, 1, 32, 64)), ("hg_s", (1, 8, 8, 128, 128)), ("re_s", (1, 8, 32, 64)), ("im_s", (1, 8, 32, 64))]


def kernel(**inputs):
    import numpy as _np
    import concourse.bacc as _bacc
    from concourse import mybir as _mybir
    from concourse.bass_utils import run_bass_kernel_spmd as _run

    nc = _bacc.Bacc("TRN2", target_bir_lowering=False, num_devices=1)
    arrays, ins, outs = {}, {}, {}
    for name in _INS:
        arr = _np.ascontiguousarray(inputs[name])
        arrays[f"in_{name}_dram"] = arr
        ins[name] = nc.dram_tensor(f"in_{name}_dram", arr.shape, _mybir.dt.from_np(arr.dtype), kind="ExternalInput").ap()
    for name, shape in _OUTS:
        outs[name] = nc.dram_tensor(f"out_{name}_dram", shape, _mybir.dt.float32, kind="ExternalOutput").ap()
    mixer_moe(nc, ins, outs)
    r = _run(nc, [arrays], core_ids=[0])
    return tuple(r.results[0][f"out_{name}_dram"] for name, _ in _OUTS)
```

```python
from contextlib import ExitStack

import numpy as np
import concourse.bass as bass
from concourse import mybir

F32 = mybir.dt.float32
I32 = mybir.dt.int32
ALU = mybir.AluOpType
ACT = mybir.ActivationFunctionType
X = mybir.AxisListType.X

P = 128
D = 1024
KD = D // P
NP_TOK, NB, SEQ_S = 256, 8, 8
NS_TOK = NB * SEQ_S
NT = NP_TOK + NS_TOK
TOK = [(0, P), (P, P), (2 * P, NS_TOK)]
HEADS, CH = 8, 64
NCH = NP_TOK // CH
GH = 4
W4 = GH * P
HG_SCALE = float(P) ** -0.5
GROUPS_S5, ST, CG = 32, 64, 16
S5W = GROUPS_S5 * CG
T5 = GROUPS_S5 * ST // P
T5Q = T5 // 4
LEVELS = 8
NX, OFF_Q, OFF_F, OFF_V, OFF_O, OFF_U, OFF_GA, OFF_GB = 6656, 0, 1024, 2048, 3072, 4096, 4608, 5632
EPS = 1e-6
NG, NE_G = 4, 8
NE = NG * NE_G
DE = 512
KE = DE // P
CAP = 64
OV = 2 * NT // (CAP + 1)
UNIT = 4096
BIG = 3.0e38
SHARE = [(6, 0), (7, 0), (5, 0), (6, 0), (7, 0), (7, NS_TOK)]
SHARED = [1, 2, 3, 4, 6, 6]
SHARE_AFTER = [0, 0, 0, 1, 2, 2]

UNITS = ["u", "f0", "q0", "v0", "q1", "f1", "v1", "o0", "o1", "gb0", "gb1", "za", "zg", "ga0", "wa0",
         "ga1", "wa1", "wo0", "wo1"]
MIX_SLOTS = 3
SLOT = {u: n % MIX_SLOTS for n, u in enumerate(UNITS)}
TURN = {u: n // MIX_SLOTS for n, u in enumerate(UNITS)}
USED = [sum(SLOT[u] == s for u in UNITS) for s in range(MIX_SLOTS)] + [1] * 5
UP_SLOT, DOWN_SLOT = [5, 1], [2, 0]
GATE_SLOT = [[3, 4], [6, 7]]


def schedule():
    proj = lambda *units: [("proj", u, j) for u in units for j in range(3 if u[0] == "v" else 4)]
    heads = lambda g: [[("o", g, 0)]] + [[("dss", g, h - 1, 0), ("dss", g, h - 1, 1), ("mean", g, h - 1), ("o", g, h)]
                                         for h in range(1, GH)] + \
        [[("dss", g, GH - 1, 0), ("dss", g, GH - 1, 1), ("mean", g, GH - 1)]]
    front = lambda g: [[("kn", g, i) for i in range(3)], [("sc", g, i) for i in range(3)],
                       [("ds", g, 0), ("ds", g, 1)], [("ds", g, 2), ("ds", g, 3)]]
    steps = [("xt", i, h) for i in range(3) for h in range(2)]
    steps += proj("u")[0:2] + [("params",)] + proj("u")[2:] + proj("f0") + [("h0",), ("bt", 0), ("bt", 1), ("ct", 0), ("ct", 1)]
    main = proj("q0", "v0", "q1", "f1", "v1", "o0", "o1", "gb0", "gb1")
    behind = {p: [] for p in main}
    behind[("proj", "q0", 0)] += [("log", 0)]
    behind[("proj", "q0", 3)] += [("exp", 0)]
    behind[("proj", "v0", 0)] += [("decay", 0)]
    for p, x in zip(proj("q1"), front(0)):
        behind[p] += x
    for p, x in zip(proj("f1", "v1"), heads(0)):
        behind[p] += x
    behind[("proj", "v1", 0)] += [("log", 1)]
    behind[("proj", "v1", 1)] += [("exp", 1)]
    behind[("proj", "v1", 2)] += [("decay", 1)]
    for p, x in zip(proj("o0"), front(1)):
        behind[p] += x
    for p, x in zip(proj("o1", "gb0"), heads(1)):
        behind[p] += x
    for g in range(2):
        order = proj("f1", "v1") if g == 0 else proj("o1", "gb0")
        for h in range(GH):
            behind[order[h + 1]] += [("st_out", GH * g + h)]
            behind[("proj", "o0", h) if g == 0 else order[h + 1]] += [("gate", GH * g + h)]
        behind[order[1]] += [("hg_p", g)]
    behind[("proj", "q1", 1)] += [("st_in", 2), ("st_in", 3)]
    behind[("proj", "v1", 1)] += [("st_in", 4), ("st_in", 5)]
    behind[("proj", "o0", 1)] += [("st_in", 6), ("st_in", 7)]
    t = 0
    for n, p in enumerate(main):
        steps += [p] + behind[p]
        if t <= T5 and n == S5_FIRST + (len(main) - 4) * t // T5:
            steps += [("bu", t)] * (t < T5) + [("sy", t - 1)] * (t > 0)
            t += 1
    while t <= T5:
        steps += [("bu", t)] * (t < T5) + [("sy", t - 1)] * (t > 0)
        t += 1
    for j in range(KD):
        steps += [("proj", "zg", j), ("proj", "za", j)]
    steps += [("states",)]
    for h in range(2):
        for j in range(4):
            steps += [("proj", f"ga{h}", j), ("proj", f"wa{h}", j)]
    mix = lambda i: [("mix", i, 0), ("mix", i, 1)]
    ht = lambda i: [("ht", i, 0), ("ht", i, 1)]
    steps += mix(0) + mix(1) + ht(0) + mix(2) + [("logits", 0)] + ht(1) + [("logits", 1)] + ht(2) + [("logits", 2)]
    steps += [("rank",)]
    return steps


S5_FIRST = 1
STEPS = schedule()


def banks():
    taken, where, turns = [0] * 8, {}, {"main": 0, "short": 0}

    def take(key, b):
        where[key] = (b, taken[b])
        taken[b] += 1

    def rotate(key, which, first, n):
        take(key, first + turns[which] % n)
        turns[which] += 1

    for st in STEPS:
        if st[0] in ("log", "exp", "decay", "st_out", "st_in", "hg_p", "gate") or st == ("mix", 2, 1):
            continue
        if st[0] == "bu":
            take(("bur",) + st[1:], 2)
            take(("bui",) + st[1:], 3)
        elif st[0] == "sy":
            if st[1] % 4 == 0:
                take(("y5", st[1] // 4), 4)
        elif st[0] == "states":
            rotate(("fs",), "short", 5, 3)
            rotate(("fss",), "short", 5, 3)
        elif st[0] in ("kn", "sc", "o", "mean", "ds", "dss"):
            rotate(st, "short", 5, 3)
        else:
            rotate(st, "main", 0, 2)
    return where


BANK = banks()
UNIT_LAST = {}
for _st in STEPS:
    if _st[0] == "proj":
        UNIT_LAST[_st[1]] = _st


def round_of(slot, turn, half):
    return turn if slot in GATE_SLOT[0] + GATE_SLOT[1] else turn * 2 + half


def mixer_moe(nc, a, o):
    ctx = ExitStack()
    with ctx:
        def sb(name, shape, dt=F32):
            return ctx.enter_context(nc.sbuf_tensor(name, shape, dt))

        def sem(name):
            return ctx.enter_context(nc.semaphore(name))

        K = 256
        arena = sb("arena", [P, 191 * K])

        def part(kib, n, pat=None, rows=P, **kw):
            v = arena[0:rows, int(kib * K):int(kib * K) + n]
            return v.rearrange(pat, **kw) if pat else v

        ring = [part(k, UNIT) for k in (0, 16, 32, 60, 76, 92, 159, 175)]
        h2 = part(48, 3 * D, "p (t d) -> p t d", t=3)
        kk = part(60, GH * NT, "p (h n) -> p h n", h=GH)
        junk = part(60, D)
        bc = part(65, GH * NT, "p (h n) -> p h n", h=GH)
        eb = part(70, GH * NT, "p (h n) -> p h n", h=GH)
        kd = part(75, GH * NT, "p (h n) -> p h n", h=GH)
        qd = part(80, GH * NT, "p (h n) -> p h n", h=GH)
        sp_ = part(85, NCH * W4, "p (c n) -> p c n", c=NCH)
        stt_ = [part(k, NB * P, "p (b v) -> p b v", b=NB) for k in (93, 97, 65, 75)]
        scp = part(101, 2 * GH * P, "p (c h t) -> p c h t", h=GH, c=2)
        scs = part(124, GH * NS_TOK, "p (h t) -> p h t", rows=NS_TOK, h=GH)
        blast = part(107.5, GH * 12, "p (h c) -> p h c", h=GH)
        eblast = part(107.75, GH * 12, "p (h c) -> p h c", h=GH)
        rstd_o = part(105, NT)
        osq = part(106.25, NT)
        vn = part(108, 3 * W4, "p (t n) -> p t n", t=3)
        kn = part(114, 3 * W4, "p (t n) -> p t n", t=3)
        vm = part(120, NB * P, "p (b v) -> p b v", rows=NS_TOK, b=NB)
        rows76 = part(108, P)
        braw = part(108.5, 2 * T5 * CG, "p (r t c) -> p r t c", r=2, t=T5)
        craw = part(110.5, 2 * 4 * ST, "p (r t s) -> p r t s", r=2, t=4)
        h0rows = part(112.5, 2 * P, "p (r s) -> p r s", r=2)
        h0t = part(113.5, 2 * P, "p (r b t) -> p r t b", r=2, b=NB)
        bd = part(114.5, 2 * T5 * 2 * CG, "p (r t q c) -> p r t q c", r=2, t=T5, q=2)
        cd = part(118.5, 2 * 4 * P, "p (r t q s) -> p r t q s", r=2, t=4, q=2)
        ptmp = part(122.5, T5 * CG, "p (t c) -> p t c", t=T5)
        ptmp2 = part(123.5, T5 * CG, "p (t c) -> p t c", t=T5)
        smask = part(125, NT)
        cosT = part(127, 2 * T5Q * NT, "p (t n) -> p t n", t=2 * T5Q)
        sinT = part(137, 2 * T5Q * NT, "p (t n) -> p t n", t=2 * T5Q)
        wr, wi, tm1, tm2 = (part(147 + 1.25 * i, NT) for i in range(4))
        gr = part(152, 2 * NT, "p (s n) -> p s n", s=2)
        gi = part(154.5, 2 * NT, "p (s n) -> p s n", s=2)
        hr = part(157, 2 * NT, "p (s n) -> p s n", s=2)
        hi = part(159.5, 2 * NT, "p (s n) -> p s n", s=2)
        pt1, pt2, rdec = (part(162 + 1.25 * i, NT) for i in range(3))
        ptab = part(162, T5Q * P)
        fstage = part(152, 2 * P, "p (r s) -> p r s", r=2)
        hT = part(166, KD * NT, "p (k n) -> p k n", k=KD)
        oT = part(176, KD * NT, "p (k n) -> p k n", k=KD)
        uT = part(186, 4 * NT, "p (k n) -> p k n", k=4)
        gy = uT
        xn = part(176, 2 * D, "p (s d) -> p s d", s=2)
        grow = part(186, D)
        merged = part(108, KD * NT, "p (k n) -> p k n", k=KD)
        sga = part(118, 2 * NT, "p (s n) -> p s n", s=2)
        sgo = part(70, 2 * NT, "p (s n) -> p s n", s=2)
        hn = part(121, 3 * D, "p (t d) -> p t d", t=3)
        pick = part(108, 3 * P, "p (t s) -> p t s", t=3)
        xT = part(110, KD * P, "p (k s) -> p k s", k=KD)
        junk_x = part(110, D)
        sil = part(114, DE)
        hid = part(116, DE)
        hidT = part(118, DE, "p (k s) -> p k s", k=KE)
        yrow = part(133, D, "p (h d) -> p h d", h=2)
        gffn = part(138, D)
        gfin = part(142, D)
        hnT = part(146, KD * NT, "p (k n) -> p k n", k=KD)
        wpick = part(146, 3 * P, "p (t s) -> p t s", t=3)
        wtmp = part(147.5, 3 * P, "p (t s) -> p t s", t=3)
        wpT = part(149, NT)
        wrt = part(156, KD * (NG + NE), "p (k e) -> p k e", k=KD)
        brt = part(158, NG + NE)
        upper = part(157.25, P)
        lg = part(137, 3 * 36, "p (t e) -> p t e", t=3)
        r32 = [part(110 + 0.375 * i, 3 * NE, "p (t g e) -> p t g e", t=3, g=NG) for i in range(8)]
        r8 = [part(113 + 0.125 * i, 3 * NE_G, "p (t e) -> p t e", t=3) for i in range(7)]
        r1 = [part(114 + 0.0625 * i, 3, "p (t e) -> p t e", t=3) for i in range(9)]
        ovj = part(115, OV * NE, "p (j e) -> p j e", j=OV)
        nE = part(116.25, NE)
        ovt = part(116.5, NE)
        incl = part(116.75, NE)
        corr = part(117, NE)
        ident = sb("ident", [P, P])
        ones = sb("ones", [P, P])
        iota_s = sb("iota_s", [P, P])
        iota_i = sb("iota_i", [P, P], I32)
        par_i = sb("par_i", [P, 2], I32)
        par = sb("par", [P, 2])
        negp = sb("negp", [P, 2])
        cmask = sb("cmask", [P, NT])
        seqm = sb("seqm", [NS_TOK, NB])
        rev = sb("rev", [P, NE])
        pcol = sb("pcol", [P, 76])
        ldt = sb("ldt", [P, GROUPS_S5])
        cf = sb("cf", [P, 19, T5])
        pw = sb("pw", [P, LEVELS, 2, T5])
        lb = sb("lb", [P, 6, HEADS])
        ah = sb("ah", [P, 2, T5, NB])
        fsp = sb("fsp", [P, 2, T5])
        fss = sb("fss", [P, 2, NB, T5])
        btr = sb("btr", [P, 2, 4, P])
        ctr = sb("ctr", [P, 2, 4, P])
        ss = sb("ss", [P, 3])
        rs = sb("rs", [P, 3, 3])
        epsc = sb("epsc", [P, 1])
        slot = sb("slot", [P, 2, 3])
        wtop = sb("wtop", [P, 2, 3])
        wslot = sb("wslot", [P, 2, 3])
        ovi = sb("ovi", [P, 16], I32)

        LBH, OML, NOML, ON, ONG = 0, 1, 2, 3, 4

        ps = [ctx.enter_context(nc.psum_tensor(f"bank{i}", [P, 512], F32)) for i in range(8)]
        x_in = [sem(f"x_in{i}") for i in range(3)]
        gmix_in = sem("gmix_in")
        small_in = sem("small_in")
        late_in = sem("late_in")
        st_in = [sem(f"st_in{i}") for i in range(4)]
        st_out = [sem(f"st_out{i}") for i in range(4)]
        full = [sem(f"unit_full{i}") for i in range(8)]
        used = [sem(f"unit_used{i}") for i in range(8)]
        filled = [sem(f"bank_filled{i}") for i in range(8)]
        emptied = [sem(f"bank_emptied{i}") for i in range(8)]
        names = ["consts", "cp_done", "ss_done", "rstd_done", "xn_done", "dt_exp", "mag_exp", "mag_in", "phasor",
                 "lb_in", "lb_exp", "lb_done", "bdcd", "tab_done", "k_done", "logf", "scan_done",
                 "exp_done", "diff_done", "dexp", "kd_done", "qd_done", "kl_done", "kn_done",
                 "sc_raw", "sc_done", "state_new", "o_raw", "vm_done", "st_sum", "g_done", "h_done",
                 "h_used", "y5_ev", "gy_done", "v_done", "sq_done", "o_final", "sig_a", "sig_g",
                 "sil_o", "merged_ok", "yb_done", "u_done", "fs_done", "fst_done", "out_done",
                 "h2_done", "ss2", "hn_done", "hnT_done", "mats", "gexp_in", "gexp", "slots",
                 "pick_done", "xT_done", "sel_done", "on_done", "f_done", "q_done", "fin_sum",
                 "fin_done", "y_out", "dve", "pool", "act", "ov_w", "ov_ss", "ov_p", "ov_sel", "ov_x",
                 "ov_g", "ov_u", "ov_sil", "ov_hid", "ov_dn", "ov_y", "ov_t", "ov_hidT",
                 "silu_done", "hid_done", "hidT_ready", "hidT_done", "y_copied", "upper_done",
                 "sig_b", "y_b", "y_a", "dve_end", "hr_done", "v_half", "no_rows", "wpick_done",
                 "wpT_ready", "wpT_done", "shared", "added", "ov_wp", "ov_wT", "ov_wpT", "ov_sh",
                 "ov_add"]
        S = {n: sem(n) for n in names}

        x_tok = [a["x_prompt"][0, 0:P, :], a["x_prompt"][0, P:2 * P, :],
                 a["x_sample"].rearrange("b s d -> (b s) d")]
        w_in = a["w_in"][0]
        sthg = a["state_hgrn"][0]

        def bcast_rows(v, n):
            return v.rearrange("(o d) -> o d", o=1).broadcast_to([n, v.shape[0]])

        def unit_src(u):
            if u in ("wo0", "wo1"):
                c = 512 * int(u[2])
                return a["w_out"][0][:, c:c + 512].rearrange("(k p) n -> p k n", p=P)
            if u in ("wa0", "wa1"):
                c = 512 * int(u[2])
                return a["w_branch_a"][0][:, c:c + 512].rearrange("(k p) n -> p k n", p=P)
            if u in ("za", "zg"):
                c = D * (u == "zg")
                return a["w_glu"][0][:, c:c + D].rearrange("(k p) n -> p k n", p=P)
            base = {"u": OFF_U, "f0": OFF_F, "q0": OFF_Q, "v0": OFF_V, "f1": OFF_F + 512, "q1": OFF_Q + 512,
                    "v1": OFF_V + 512, "o0": OFF_O, "o1": OFF_O + 512, "ga0": OFF_GA, "ga1": OFF_GA + 512,
                    "gb0": OFF_GB, "gb1": OFF_GB + 512}[u]
            return w_in[:, base:base + 512].rearrange("(k p) n -> p k n", p=P)

        def unit_view(u, kt=KD):
            return ring[SLOT[u]].rearrange("p (k n) -> p k n", k=4 if u in ("za", "zg") else KD)

        wg_d, wu_d, wd_d = a["w_exp_gate"][0], a["w_exp_up"][0], a["w_exp_down"][0]

        def bank(key, n=512, rows=P):
            return ps[BANK[key][0]][0:rows, 0:n]

        def wait_filled(eng, key):
            b, n = BANK[key]
            eng.wait_ge(filled[b], n + 1)

        def wait_emptied(eng, key):
            b, n = BANK[key]
            if n:
                eng.wait_ge(emptied[b], n)

        def is_filled(ins, key):
            ins.then_inc(filled[BANK[key][0]], 1)

        def is_emptied(ins, key):
            ins.then_inc(emptied[BANK[key][0]], 1)

        def bt(v, n, at=None):
            return v.unsqueeze(len(v.shape)).broadcast_to(list(v.shape) + [n])

        block = ctx.enter_context(nc.Block())

        @block.sync
        def _(sp):
            for i, (t0, n) in enumerate(TOK):
                sp.dma_start(h2[0:n, i, :], x_tok[i]).then_inc(x_in[i], 16)
                if i == 0:
                    sp.dma_start(grow, bcast_rows(a["norm_mix_g"][0], P)).then_inc(gmix_in, 16)

            def small_parameters():
                dm = lambda dst, src: sp.dma_start(dst, src).then_inc(small_in, 16)
                dm(rows76[16:24, :], a["hgrn_onorm_g"][0])
                dm(rows76[24:40, :], a["b_glu"][0].rearrange("(h k) -> h k", k=P))
                dm(rows76[40:44, :], a["s5_d"][0].rearrange("(h k) -> h k", k=P))
                for r, nme in enumerate(("s5_b_re", "s5_b_im")):
                    dm(braw[:, r], a[nme][0].rearrange("(t q) s c -> (q s) t c", q=2))
                for r, nme in enumerate(("s5_c_re", "s5_c_im")):
                    dm(craw[:, r], a[nme][0].rearrange("(t g) c s -> (g c) t s", t=4))
                for r, nme in enumerate(("state_s5_re", "state_s5_im")):
                    dm(h0rows[:, r], a[nme][0].rearrange("b (t q) s -> (b t) (q s)", q=2))

            def late_parameters():
                dm = lambda dst, src: sp.dma_start(dst, src).then_inc(late_in, 16)
                sp.wait_ge(S["h_used"], T5)
                sp.wait_ge(S["fs_done"], T5)
                dm(wrt[:, :, 0:NG], a["w_router_group"][0].rearrange("(p k) e -> p k e", p=P))
                for g in range(NG):
                    dm(wrt[:, :, NG + NE_G * g:NG + NE_G * (g + 1)],
                       a["w_router_expert"][0, g].rearrange("(p k) e -> p k e", p=P))
                dm(brt[:, 0:NG], bcast_rows(a["b_router_group"][0], P))
                dm(brt[:, NG:], bcast_rows(a["b_router_expert"][0].rearrange("g e -> (g e)"), P))
                dm(gffn, bcast_rows(a["norm_ffn_g"][0], P))
                dm(gfin, bcast_rows(a["norm_final_g"], P))

            for n, u in enumerate(UNITS):
                if TURN[u]:
                    sp.wait_ge(used[SLOT[u]], TURN[u])
                sp.dma_start(ring[SLOT[u]].rearrange("p (k n) -> p k n", k=4 if u in ("za", "zg") else KD),
                             unit_src(u)).then_inc(full[SLOT[u]], 16)
                if u == "u":
                    small_parameters()
                if u == "v0":
                    for h in range(2):
                        sp.dma_start(stt_[h], sthg[:, h, :, :].rearrange("b k v -> k b v")).then_inc(
                            st_in[h], 16)
                if u == "wa1":
                    late_parameters()
            for h in range(4):
                sp.wait_ge(st_out[h], 2 * 16)
            sp.wait_ge(S["out_done"], 32)
            sp.wait_ge(S["o_final"], HEADS)
            with sp.Fori(0, NE // 4) as turn:
                for half in range(2):
                    it = turn * 2 + half
                    for slots, src in ((GATE_SLOT[half], wg_d), (UP_SLOT, wu_d), (DOWN_SLOT, wd_d)):
                        for e, s in enumerate(slots):
                            sp.wait_ge(used[s], round_of(s, turn, half) + USED[s])
                            sp.dma_start(ring[s], src[bass.ds(it * 2 + e, 1), :, :].rearrange(
                                "o (p k) n -> p (o k n)", p=P)).then_inc(full[s], 16)
            sp.wait_ge(S["slots"], 1)
            n_ov = sp.value_load(ovi[0:1, 15:16], min_val=0, max_val=OV)
            with sp.If(n_ov > 0):
                for s in range(3):
                    sp.wait_ge(used[s], USED[s] + NE // 2)
                with sp.Fori(0, n_ov) as j:
                    sp.wait_ge(S["ov_dn"], j + 1)
                    ex = sp.value_load(ovi[0:1, bass.ds(j, 1)], min_val=0, max_val=NE - 1)
                    for s, src in enumerate((wg_d, wu_d, wd_d)):
                        sp.dma_start(ring[s], src[bass.ds(ex, 1), :, :].rearrange(
                            "o (p k) n -> p (o k n)", p=P)).then_inc(S["ov_w"], 16)
            for i, (t0, n) in enumerate(TOK):
                sp.wait_ge(S["fin_done"], i + 1)
                dst = o["y_p"][0, t0:t0 + n, :] if i < 2 else o["y_s"].rearrange("b s d -> (b s) d")
                sp.dma_start(dst, h2[0:n, i, :]).then_inc(S["y_out"], 16)
            sp.wait_ge(S["y_out"], 48)
            sp.wait_ge(S["fst_done"], 6 * 16)

        @block.tensor
        def _(pe):
            mm = nc.tensor.matmul
            pe.wait_ge(S["consts"], 1)
            s5_waited = False
            for st in STEPS:
                kind = st[0]
                if kind == "params":
                    pe.wait_ge(small_in, 13 * 16)
                    wait_emptied(pe, st)
                    is_filled(nc.tensor.transpose(bank(st, 76), rows76[0:76, :], ident[0:76, 0:76]), st)
                elif kind in ("xt", "ht"):
                    _, i, h = st
                    n = TOK[i][1]
                    pe.wait_ge(S["xn_done" if kind == "xt" else "hn_done"], i + 1)
                    wait_emptied(pe, st)
                    src = xn[:, i % 2, :] if kind == "xt" else hn[:, i, :]
                    for k in range(4):
                        c = (4 * h + k) * P
                        last = nc.tensor.transpose(ps[BANK[st][0]][:, k * n:(k + 1) * n], src[0:n, c:c + P],
                                                   ident[0:n, 0:n])
                    is_filled(last, st)
                elif kind == "h0":
                    wait_emptied(pe, st)
                    for r in range(2):
                        last = nc.tensor.transpose(ps[BANK[st][0]][:, r * P:(r + 1) * P], h0rows[:, r, :], ident[:, :])
                    is_filled(last, st)
                elif kind in ("bt", "ct"):
                    r = st[1]
                    pe.wait_ge(S["bdcd"], 2 if kind == "bt" else 4)
                    wait_emptied(pe, st)
                    for T in range(4):
                        src = bd[:, r, 4 * T:4 * T + 4, :, :].rearrange("p t q c -> p (t q c)") if kind == "bt" else \
                            cd[:, r, T, :, :].rearrange("p q s -> p (q s)")
                        last = nc.tensor.transpose(ps[BANK[st][0]][:, T * P:(T + 1) * P], src, ident[:, :])
                    is_filled(last, st)
                elif kind == "proj":
                    _, u, j = st
                    pe.wait_ge(full[SLOT[u]], 16 * (TURN[u] + 1))
                    wait_emptied(pe, st)
                    w = unit_view(u)
                    kt = 4 if u in ("za", "zg") else KD
                    if u == "u" and j == 0:
                        pe.wait_ge(S["cp_done"], 6)
                    if u == "wa0" and j == 0:
                        pe.wait_ge(S["o_final"], HEADS)
                    if u == "zg" and j == 0:
                        pe.wait_ge(S["gy_done"], 4)
                    if u == "ga0" and j == 0:
                        for s in (3, 4, 5):
                            pe.sem_inc(used[s], 1)
                    act = {"wa": oT, "za": gy, "zg": gy}.get(u[0:2], hT)
                    if u[0] == "v":
                        t0, n = TOK[j]
                        for k in range(kt):
                            if n == P:
                                last = mm(bank(st), hT[:, k, t0:t0 + n], w[:, k, :], start=k == 0, stop=k == kt - 1)
                                continue
                            for c in range(2):
                                last = mm(bank(st)[n * c:n * (c + 1), 0:256], hT[:, k, t0:t0 + n],
                                          w[:, k, 256 * c:256 * (c + 1)], start=k == 0, stop=k == kt - 1)
                    else:
                        for k in range(kt):
                            last = mm(bank(st, NT), w[:, k, j * P:(j + 1) * P], act[:, k, :], start=k == 0,
                                      stop=k == kt - 1)
                    is_filled(last, st)
                    if UNIT_LAST[u] == st:
                        pe.wait_ge(filled[BANK[st][0]], BANK[st][1] + 1)
                        pe.sem_inc(used[SLOT[u]], 1)
                elif kind == "bu":
                    t = st[1]
                    if not s5_waited:
                        pe.wait_ge(S["u_done"], 4)
                        pe.wait_ge(S["bdcd"], 8)
                        s5_waited = True
                    for r, key in enumerate((("bur", t), ("bui", t))):
                        wait_emptied(pe, key)
                        j = 32 * (t % 4)
                        is_filled(mm(bank(key, NT), btr[j:j + 32, r, t // 4, :], uT[j:j + 32, t // 4, :],
                                     start=True, stop=True), key)
                elif kind == "sy":
                    t = st[1]
                    key = ("y5", t // 4)
                    if t % 4 == 0:
                        wait_emptied(pe, key)
                    pe.wait_ge(S["hr_done"], t + 1)
                    pe.wait_ge(S["h_done"], t + 1)
                    j = 32 * (t % 4)
                    mm(ps[4][j:j + 32, 0:NT], ctr[:, 0, t // 4, j:j + 32], hr[:, t % 2, :], start=True, stop=False)
                    last = mm(ps[4][j:j + 32, 0:NT], ctr[:, 1, t // 4, j:j + 32], hi[:, t % 2, :], start=False, stop=True)
                    last.then_inc(S["h_used"], 1)
                elif kind == "kn":
                    _, g, i = st
                    t0, n = TOK[i]
                    pe.wait_ge(S["kl_done"], g + 1)
                    wait_emptied(pe, st)
                    for h in range(GH):
                        last = nc.tensor.transpose(ps[BANK[st][0]][0:n, h * P:(h + 1) * P], bc[:, h, t0:t0 + n], ident[:, :])
                    is_filled(last, st)
                elif kind == "sc":
                    _, g, i = st
                    wait_emptied(pe, st)
                    pe.wait_ge(S["qd_done"], g + 1)
                    pe.wait_ge(S["kd_done"], g + 1)
                    b = ps[BANK[st][0]]
                    for h in range(GH):
                        if i < 2:
                            last = mm(b[:, h * P:(h + 1) * P], kd[:, h, i * P:(i + 1) * P], qd[:, h, i * P:(i + 1) * P],
                                      start=True, stop=True)
                        else:
                            last = mm(b[0:NS_TOK, h * NS_TOK:(h + 1) * NS_TOK], kd[:, h, NP_TOK:NT], qd[:, h, NP_TOK:NT],
                                      start=True, stop=True)
                    is_filled(last, st)
                elif kind == "ds":
                    _, g, c = st
                    wait_emptied(pe, st)
                    pe.wait_ge(S["kn_done"], 3 * (g + 1))
                    pe.wait_ge(S["v_done"], 3 * (g + 1))
                    r = CH * (c % 2)
                    for h in range(GH):
                        last = mm(bank(st)[:, h * P:(h + 1) * P], kn[r:r + CH, c // 2, h * P:(h + 1) * P],
                                  vn[r:r + CH, c // 2, h * P:(h + 1) * P], start=True, stop=True)
                    is_filled(last, st)
                elif kind == "dss":
                    _, g, h, i = st
                    wait_emptied(pe, st)
                    pe.wait_ge(S["vm_done"], GH * g + h + 1)
                    is_filled(mm(bank(st), kn[0:NS_TOK, 2, h * P:(h + 1) * P],
                                 vm[:, 4 * i:4 * i + 4, :].rearrange("p b v -> p (b v)"), start=True, stop=True), st)
                elif kind == "o":
                    _, g, h = st
                    wait_emptied(pe, st)
                    pe.wait_ge(S["sc_done"], 3 * (g + 1))
                    pe.wait_ge(S["state_new"], NCH * (g + 1))
                    pe.wait_ge(st_in[h], 16 * (g + 1))
                    b = ps[BANK[st][0]]
                    for c in range(2):
                        mm(b[:, c * P:(c + 1) * P], vn[:, c, h * P:(h + 1) * P], scp[:, c, h, :], start=True, stop=True)
                        for cc in range(max(2 * c, 1), 2 * c + 2):
                            s = CH * cc
                            mm(b[:, s:s + CH], sp_[:, cc - 1, h * P:(h + 1) * P], qd[:, h, s:s + CH], start=False,
                               stop=True, skip_group_check=True)
                    mm(b[:, NP_TOK:NT], vn[0:NS_TOK, 2, h * P:(h + 1) * P], scs[:, h, :], start=True, stop=True)
                    for q in range(NB):
                        s = NP_TOK + SEQ_S * q
                        last = mm(b[:, s:s + SEQ_S], stt_[h][:, q, :], qd[:, h, s:s + SEQ_S], start=False,
                                  stop=True, skip_group_check=True)
                    is_filled(last, st)
                elif kind == "mean":
                    _, g, h = st
                    wait_emptied(pe, st)
                    pe.wait_ge(S["sq_done"], GH * g + h + 1)
                    is_filled(mm(bank(st, NT), ones[:, :], osq, start=True, stop=True), st)
                elif kind == "states":
                    pe.wait_ge(S["fs_done"], T5)
                    for key, n in ((("fs",), 1), (("fss",), NB)):
                        wait_emptied(pe, key)
                        for r in range(2):
                            src = fsp[:, r, :] if n == 1 else fss[:, r].rearrange("p b t -> p (b t)")
                            if n == 1:
                                last = nc.tensor.transpose(ps[BANK[key][0]][0:T5, r * P:(r + 1) * P], src, ident[:, :])
                            else:
                                last = nc.tensor.transpose(ps[BANK[key][0]][:, r * P:(r + 1) * P], src, ident[:, :])
                        is_filled(last, key)
                elif kind == "mix":
                    _, i, h = st
                    t0, n = TOK[i]
                    if i == h == 0:
                        wait_filled(pe, ("proj", "wa1", 3))
                        for s in (6, 7):
                            pe.sem_inc(used[s], 1)
                        pe.wait_ge(S["merged_ok"], KD)
                    if (i, h) == (2, 1):
                        continue
                    halves = (h,) if n == P else (0, 1)
                    for c in halves:
                        pe.wait_ge(full[SLOT[f"wo{c}"]], 16 * (TURN[f"wo{c}"] + 1))
                    wait_emptied(pe, st)
                    for k in range(KD):
                        for c in halves:
                            r = 0 if n == P else n * c
                            last = mm(bank(st)[r:r + n, :], merged[:, k, t0:t0 + n], unit_view(f"wo{c}")[:, k, :],
                                      start=k == 0, stop=k == KD - 1)
                    is_filled(last, st)
                    if i == 2:
                        pe.wait_ge(filled[BANK[st][0]], BANK[st][1] + 1)
                        for c in range(2):
                            pe.sem_inc(used[SLOT[f"wo{c}"]], 1)
                elif kind == "logits":
                    i = st[1]
                    t0, n = TOK[i]
                    pe.wait_ge(late_in, 9 * 16)
                    pe.wait_ge(S["hnT_done"], 2 * i + 2)
                    wait_emptied(pe, st)
                    for k in range(KD):
                        last = mm(bank(st, NG + NE, n), hnT[:, k, t0:t0 + n], wrt[:, k, :], start=k == 0, stop=k == KD - 1)
                    is_filled(last, st)
                elif kind == "rank":
                    pe.wait_ge(S["upper_done"], 1)
                    pe.wait_ge(S["mats"], 1)
                    wait_emptied(pe, st)
                    M = r32[2]
                    b = ps[BANK[st][0]]
                    for i in range(4):
                        for j in range(min(i, 3)):
                            last = mm(b[:, NE * i:NE * (i + 1)], ones[:, :], M[:, j].rearrange("p g e -> p (g e)"),
                                      start=j == 0, stop=i == 3 and j == 2)
                        if i < 3:
                            last = mm(b[:, NE * i:NE * (i + 1)], upper[:, :], M[:, i].rearrange("p g e -> p (g e)"),
                                      start=i == 0, stop=True)
                    is_filled(last, st)

            def select(width):
                for k in range(KD):
                    for i, (t0, n) in enumerate(TOK):
                        last = mm(ps[k // 4][:, (k % 4) * P:(k % 4) * P + width], hn[0:n, i, k * P:(k + 1) * P],
                                  pick[0:n, i, 0:width], start=i == 0, stop=i == 2)
                return last

            def turn_wpick():
                for i, (t0, n) in enumerate(TOK):
                    last = nc.tensor.transpose(ps[5][:, t0:t0 + n], wpick[0:n, i, :], ident[0:n, 0:n])
                return last

            def share(c):
                t0, n = TOK[c // 2]
                b, r = SHARE[c]
                return mm(ps[b][r:r + n, :], wpT[:, t0:t0 + n], yrow[:, c % 2, :], start=True, stop=True)

            pe.wait_ge(emptied[BANK[("rank",)][0]], BANK[("rank",)][1] + 1)
            with pe.Fori(0, NE // 4) as turn:
                for half in range(2):
                    it = turn * 2 + half

                    def shares():
                        pe.wait_ge(S["wpT_done"], it + 1)
                        pe.wait_ge(S["y_copied"], it * 2 + 1)
                        for c in range(6):
                            if SHARE_AFTER[c]:
                                pe.wait_ge(S["added"], it * 6 + SHARE_AFTER[c])
                            share(c).then_inc(S["shared"], 1)

                    if half == 0:
                        pe.wait_ge(S["pick_done"], it + 1)
                        select(P).then_inc(S["sel_done"], 1)
                    pe.wait_ge(S["xT_done"], it + 1)
                    for slots, b in ((GATE_SLOT[half], 2), (UP_SLOT, 3)):
                        for s in slots:
                            pe.wait_ge(full[s], round_of(s, turn, half) * 16 + 16 * (USED[s] + (s < 3)))
                        pe.wait_ge(S["hid_done"], it + 1)
                        for k in range(KD):
                            for e, s in enumerate(slots):
                                last = mm(ps[b][e * CAP:(e + 1) * CAP, :], xT[:, k, e * CAP:(e + 1) * CAP],
                                          ring[s][:, k * DE:(k + 1) * DE], start=k == 0, stop=k == KD - 1)
                                if k == KD - 1:
                                    last.then_inc(used[s], 1)
                        if half == 1 and b == 2:
                            shares()
                    if half == 0:
                        pe.wait_ge(S["pick_done"], it + 2)
                        select(P).then_inc(S["sel_done"], 1)
                    pe.wait_ge(S["hid_done"], it + 2)
                    for m in range(KE):
                        last = nc.tensor.transpose(ps[4][:, m * P:(m + 1) * P], hid[:, m * P:(m + 1) * P], ident[:, :])
                    last.then_inc(S["hidT_ready"], 1)
                    if half == 0:
                        shares()
                    for s in DOWN_SLOT:
                        pe.wait_ge(full[s], round_of(s, turn, half) * 16 + 16 * (USED[s] + (s < 3)))
                    pe.wait_ge(S["hidT_done"], it + 1)
                    for h in range(2):
                        pe.wait_ge(S["added"], it * 6 + (4, 6)[h])
                        for k in range(KE):
                            for e, s in enumerate(DOWN_SLOT):
                                last = mm(ps[6 + h][e * CAP:(e + 1) * CAP, :], hidT[:, k, e * CAP:(e + 1) * CAP],
                                          ring[s][:, k * D + 512 * h:k * D + 512 * (h + 1)], start=k == 0, stop=k == KE - 1)
                                if h == 1 and k == KE - 1:
                                    last.then_inc(used[s], 1)
                    pe.wait_ge(S["wpick_done"], it + 1)
                    pe.wait_ge(S["added"], it * 6 + 6)
                    turn_wpick().then_inc(S["wpT_ready"], 1)
            pe.wait_ge(S["wpT_done"], NE // 2 + 1)
            pe.wait_ge(S["y_copied"], NE + 1)
            for c in range(6):
                if SHARE_AFTER[c]:
                    pe.wait_ge(S["added"], 6 * (NE // 2) + SHARE_AFTER[c])
                share(c).then_inc(S["shared"], 1)
            n_ov = pe.value_load(ovi[0:1, 15:16], min_val=0, max_val=OV)
            with pe.If(n_ov > 0):
                pe.wait_ge(S["xT_done"], NE // 2)
                pe.wait_ge(S["added"], 6 * (NE // 2 + 1))
                pe.sem_inc(S["ov_dn"], 1)
                with pe.Fori(0, n_ov) as j:
                    pe.wait_ge(S["ov_p"], j + 1)
                    select(CAP).then_inc(S["ov_sel"], 1)
                    pe.wait_ge(S["ov_x"], j + 1)
                    pe.wait_ge(S["ov_w"], j * 48 + 48)
                    for w, name in enumerate(("ov_g", "ov_u")):
                        for k in range(KD):
                            last = mm(ps[2 + w][0:CAP, :], xT[:, k, 0:CAP], ring[w][:, k * DE:(k + 1) * DE],
                                      start=k == 0, stop=k == KD - 1)
                        last.then_inc(S[name], 1)
                    pe.wait_ge(S["ov_wp"], j + 1)
                    turn_wpick().then_inc(S["ov_wT"], 1)
                    pe.wait_ge(S["ov_hid"], j + 1)
                    for m in range(KE):
                        last = nc.tensor.transpose(ps[4][:, m * P:(m + 1) * P], hid[:, m * P:(m + 1) * P], ident[:, :])
                    last.then_inc(S["ov_t"], 1)
                    pe.wait_ge(S["ov_hidT"], j + 1)
                    for h in range(2):
                        for k in range(KE):
                            last = mm(ps[6 + h][0:CAP, :], hidT[:, k, 0:CAP],
                                      ring[2][:, k * D + 512 * h:k * D + 512 * (h + 1)], start=k == 0, stop=k == KE - 1)
                    last.then_inc(S["ov_dn"], 1)
                    pe.wait_ge(S["ov_wpT"], j + 1)
                    pe.wait_ge(S["ov_y"], j * 2 + 2)
                    for c in range(6):
                        if SHARE_AFTER[c]:
                            pe.wait_ge(S["ov_add"], j * 6 + SHARE_AFTER[c])
                        share(c).then_inc(S["ov_sh"], 1)
                    pe.wait_ge(S["ov_add"], j * 6 + 6)

        @block.scalar
        def _(act):
            ac = nc.scalar.activation
            cnt = [0]

            def link(ins):
                cnt[0] += 1
                ins.then_inc(S["act"], 1)
                act.wait_ge(S["act"], cnt[0])

            dm = lambda dst, src: act.dma_start(dst, src).then_inc(small_in, 16)
            dm(rows76[0:16, :], a["hgrn_lb_raw"].rearrange("r (h k) -> (r h) k", k=P))
            dm(rows76[44:60, :], a["s5_lambda_re"][0].rearrange("(t q) s -> t (q s)", q=2))
            dm(rows76[60:76, :], a["s5_lambda_im"][0].rearrange("(t q) s -> t (q s)", q=2))
            dm(ldt[:, :], bcast_rows(a["s5_log_dt"][0], P))
            act.wait_ge(S["consts"], 1)
            for i, (t0, n) in enumerate(TOK):
                act.wait_ge(x_in[i], 16)
                if i:
                    act.wait_ge(S["ss_done"], i)
                ac(junk[0:n, :], h2[0:n, i, :], ACT.Square, accum_out=ss[0:n, i:i + 1]).then_inc(S["ss_done"], 1)
            for st in STEPS:
                kind = st[0]
                if kind in ("xt", "ht"):
                    _, i, h = st
                    t0, n = TOK[i]
                    wait_filled(act, st)
                    if st == ("ht", 0, 0):
                        act.wait_ge(S["fst_done"], 6 * 16)
                    dst = (hT if kind == "xt" else hnT)[:, 4 * h:4 * h + 4, t0:t0 + n]
                    nc.scalar.copy(dst, bank(st, 4 * n).rearrange("p (k n) -> p k n", k=4)).then_inc(
                        S["cp_done" if kind == "xt" else "hnT_done"], 1)
                    act.wait_ge(S["cp_done" if kind == "xt" else "hnT_done"], 2 * i + h + 1)
                    act.sem_inc(emptied[BANK[st][0]], 1)
                elif kind == "params":
                    act.wait_ge(small_in, 13 * 16)
                    for q in range(2):
                        ac(cf[ST * q:ST * (q + 1), 0, :], ldt[ST * q:ST * (q + 1), q:GROUPS_S5:2], ACT.Exp).then_inc(
                            S["dt_exp"], 1)
                    act.wait_ge(S["mag_in"], 1)
                    ac(cf[:, 3, :], cf[:, 1, :], ACT.Exp).then_inc(S["mag_exp"], 1)
                    act.wait_ge(S["lb_in"], 1)
                    ac(lb[:, 0:2, :], lb[:, 0:2, :], ACT.Exp).then_inc(S["lb_exp"], 1)
                elif kind == "proj":
                    _, u, j = st
                    if u == "u":
                        wait_filled(act, st)
                        nc.scalar.copy(uT[:, j, :], bank(st, NT)).then_inc(S["u_done"], 1)
                        act.wait_ge(S["u_done"], j + 1)
                        act.sem_inc(emptied[BANK[st][0]], 1)
                    elif u[0] == "f":
                        g = int(u[1])
                        wait_filled(act, st)
                        if g:
                            act.wait_ge(S["kl_done"], g)
                        ac(kk[:, j, :], bank(st, NT), ACT.Sigmoid).then_inc(S["f_done"], 1)
                        act.wait_ge(S["f_done"], GH * g + j + 1)
                        act.sem_inc(emptied[BANK[st][0]], 1)
                    elif u[0] == "v":
                        g, n = int(u[1]), TOK[j][1]
                        wait_filled(act, st)
                        if g and j == 0:
                            act.wait_ge(filled[BANK[("o", 0, GH - 1)][0]], BANK[("o", 0, GH - 1)][1] + 1)
                            act.wait_ge(S["vm_done"], GH)
                        if n == NS_TOK:
                            nc.scalar.copy(vn[0:n, j, 256:512], bank(st)[n:2 * n, 0:256]).then_inc(S["v_half"], 1)
                            act.wait_ge(S["v_half"], g + 1)
                            nc.scalar.copy(vn[0:n, j, 0:256], bank(st)[0:n, 0:256]).then_inc(S["v_done"], 1)
                        else:
                            nc.scalar.copy(vn[0:n, j, :], bank(st)).then_inc(S["v_done"], 1)
                        act.wait_ge(S["v_done"], 3 * g + j + 1)
                        act.sem_inc(emptied[BANK[st][0]], 1)
                    elif u[0] == "o":
                        h = GH * int(u[1]) + j
                        wait_filled(act, st)
                        if h == 0:
                            act.wait_ge(S["qd_done"], 2)
                            act.wait_ge(S["diff_done"], 2)
                        if h >= 2:
                            act.wait_ge(S["o_final"], h - 1)
                        ac(sgo[:, h % 2, :], bank(st, NT), ACT.Silu).then_inc(S["sil_o"], 1)
                        act.wait_ge(S["sil_o"], h + 1)
                        act.sem_inc(emptied[BANK[st][0]], 1)
                    elif u[0:2] == "gb":
                        m = 4 * int(u[2]) + j
                        wait_filled(act, st)
                        if m == 0:
                            act.wait_ge(filled[BANK[("o", 1, GH - 1)][0]], BANK[("o", 1, GH - 1)][1] + 1)
                            act.wait_ge(S["vm_done"], HEADS)
                        if m == 1:
                            act.wait_ge(S["st_sum"], 2 * HEADS)
                        ac(merged[:, m, :], bank(st, NT), ACT.Sigmoid).then_inc(S["sig_b"], 1)
                        act.wait_ge(S["sig_b"], m + 1)
                        act.sem_inc(emptied[BANK[st][0]], 1)
                    elif u == "zg":
                        wait_filled(act, st)
                        if j >= 2:
                            act.wait_ge(S["yb_done"], j - 1)
                        ac(sga[:, j % 2, :], bank(st, NT), ACT.Sigmoid, bias=pcol[:, 32 + j:33 + j]).then_inc(S["sig_g"], 1)
                        act.wait_ge(S["sig_g"], j + 1)
                        act.sem_inc(emptied[BANK[st][0]], 1)
                    elif u[0:2] == "ga":
                        m = 4 * int(u[2]) + j
                        wait_filled(act, st)
                        if m < 2:
                            act.wait_ge(S["yb_done"], KD - 1 + m)
                        else:
                            act.wait_ge(S["merged_ok"], m - 1)
                        ac(sga[:, m % 2, :], bank(st, NT), ACT.Sigmoid).then_inc(S["sig_a"], 1)
                        act.wait_ge(S["sig_a"], m + 1)
                        act.sem_inc(emptied[BANK[st][0]], 1)
                elif kind == "log":
                    g = st[1]
                    act.wait_ge(S["lb_done"], 1)
                    act.wait_ge(S["f_done"], GH * (g + 1))
                    if g:
                        wait_filled(act, ("kn", 0, 2))
                        act.wait_ge(st_out[2], 16)
                    for h in range(GH):
                        hh = GH * g + h
                        ac(bc[:, h, :], kk[:, h, :], ACT.Ln, bias=lb[:, LBH, hh:hh + 1],
                           scale=lb[:, OML, hh:hh + 1]).then_inc(S["logf"], 1)
                elif kind == "exp":
                    g = st[1]
                    act.wait_ge(S["scan_done"], GH * (g + 1))
                    if g:
                        act.wait_ge(S["qd_done"], 1)
                        act.wait_ge(S["st_sum"], 2 * GH)
                        wait_filled(act, ("sc", 0, 2))
                        act.wait_ge(st_out[3], 16)
                    ac(eb[:, :, :], bc[:, :, :], ACT.Exp).then_inc(S["exp_done"], 1)
                    ac(kd[:, :, :], bc[:, :, :], ACT.Exp, scale=-1.0).then_inc(S["exp_done"], 1)
                elif kind == "decay":
                    g = st[1]
                    act.wait_ge(S["diff_done"], g + 1)
                    ac(bc[:, :, :], bc[:, :, :], ACT.Exp).then_inc(S["dexp"], 1)
                elif kind == "st_out":
                    h = st[1]
                    act.wait_ge(S["st_sum"], 2 * h + 2)
                    act.dma_start(o["hg_s"][0, :, h, :, :].rearrange("b k v -> k b v"), stt_[h % 4]).then_inc(
                        st_out[h % 4], 16)
                elif kind == "st_in":
                    h = st[1]
                    if h >= 4:
                        act.wait_ge(st_out[h % 4], 16)
                    if h % 4 >= 2:
                        wait_filled(act, ("kn", h // 4, 2))
                        wait_filled(act, ("sc", h // 4, 2))
                    act.dma_start(stt_[h % 4], sthg[:, h, :, :].rearrange("b k v -> k b v")).then_inc(st_in[h % 4], 16)
                elif kind == "hg_p":
                    g = st[1]
                    act.wait_ge(S["state_new"], NCH * (g + 1))
                    act.dma_start(o["hg_p"][0, 0, GH * g:GH * (g + 1)].rearrange("h k v -> k h v"),
                                  sp_[:, NCH - 1, :].rearrange("p (h v) -> p h v", h=GH)).then_inc(S["out_done"], 16)
                elif kind == "kn":
                    _, g, i = st
                    n = TOK[i][1]
                    wait_filled(act, st)
                    nc.scalar.copy(kn[0:n, i, :], bank(st, 512, n)).then_inc(S["kn_done"], 1)
                    act.wait_ge(S["kn_done"], 3 * g + i + 1)
                    act.sem_inc(emptied[BANK[st][0]], 1)
                elif kind == "sc":
                    _, g, i = st
                    wait_filled(act, st)
                    if i < 2:
                        link(nc.scalar.copy(scp[:, i].rearrange("p h t -> p (h t)"), bank(st)))
                    else:
                        link(nc.scalar.copy(scs[:, :, :].rearrange("p h t -> p (h t)"), bank(st, 256, NS_TOK)))
                    act.sem_inc(emptied[BANK[st][0]], 1)
                    act.sem_inc(S["sc_raw"], 1)
                elif kind == "o":
                    _, g, h = st
                    hh = GH * g + h
                    wait_filled(act, st)
                    nc.scalar.copy(oT[:, hh, :], bank(st, NT)).then_inc(S["o_raw"], 1)
                    if hh:
                        wait_filled(act, ("mean", (hh - 1) // GH, (hh - 1) % GH))
                    ac(osq, bank(st, NT), ACT.Square).then_inc(S["sq_done"], 1)
                    act.wait_ge(S["o_raw"], hh + 1)
                    act.wait_ge(S["sq_done"], hh + 1)
                    act.sem_inc(emptied[BANK[st][0]], 1)
                elif kind == "mean":
                    _, g, h = st
                    hh = GH * g + h
                    wait_filled(act, st)
                    if hh:
                        act.wait_ge(S["on_done"], hh)
                    link(ac(rstd_o, bank(st, NT), ACT.Ln, scale=1.0 / P, bias=epsc[:, :]))
                    act.sem_inc(emptied[BANK[st][0]], 1)
                    ac(rstd_o, rstd_o, ACT.Exp, scale=-0.5).then_inc(S["rstd_done"], 1)
                elif kind == "sy" and st[1] % 4 == 3:
                    T = st[1] // 4
                    act.wait_ge(S["y5_ev"], T + 1)
                    ac(gy[:, T, :], gy[:, T, :], ACT.Gelu_apprx_tanh).then_inc(S["gy_done"], 1)
                elif kind == "states":
                    wait_filled(act, ("fs",))
                    link(nc.scalar.copy(fstage[0:T5, 0:2, :].rearrange("p r s -> p (r s)"), bank(("fs",), 2 * P, T5)))
                    act.sem_inc(emptied[BANK[("fs",)][0]], 1)
                    for r, key in enumerate(("re_p", "im_p")):
                        act.dma_start(o[key][0, 0].rearrange("(t q) s -> t (q s)", q=2), fstage[0:T5, r, :]).then_inc(
                            S["fst_done"], 16)
                    act.wait_ge(S["fst_done"], 32)
                    wait_filled(act, ("fss",))
                    link(nc.scalar.copy(fstage[:, 0:2, :].rearrange("p r s -> p (r s)"), bank(("fss",), 2 * P)))
                    act.sem_inc(emptied[BANK[("fss",)][0]], 1)
                    for r, key in enumerate(("re_s", "im_s")):
                        act.dma_start(o[key][0].rearrange("b (t q) s -> (b t) (q s)", q=2), fstage[:, r, :]).then_inc(
                            S["fst_done"], 32)
                elif kind == "mix" and st[2] == 1:
                    i = st[1]
                    n = TOK[i][1]
                    act.wait_ge(S["h2_done"], 2 * i + 2)
                    ac(hn[0:n, i, :], h2[0:n, i, :], ACT.Square, accum_out=ss[0:n, i:i + 1]).then_inc(S["ss2"], 1)
            act.wait_ge(S["gexp_in"], 1)
            ac(r32[3][:, :, 0, 0:NG], r32[3][:, :, 0, 0:NG], ACT.Exp).then_inc(S["gexp"], 1)
            ac(r1[8], r1[8], ACT.Exp).then_inc(S["gexp"], 1)
            act.wait_ge(S["no_rows"], 1)
            act.sem_inc(S["y_copied"], 1)
            act.sem_inc(S["wpT_done"], 1)
            with act.Fori(0, NE // 4) as turn:
                for half in range(2):
                    it = turn * 2 + half
                    for s in GATE_SLOT[half]:
                        act.wait_ge(used[s], round_of(s, turn, half) + (USED[s] + 1))
                    ac(sil, ps[2][:, :], ACT.Silu).then_inc(S["silu_done"], 1)
                    act.wait_ge(S["hidT_ready"], it + 1)
                    nc.scalar.copy(hidT[:, :, :], ps[4][:, :].rearrange("p (k s) -> p k s", k=KE)).then_inc(S["hidT_done"], 1)
                    for s in DOWN_SLOT:
                        act.wait_ge(used[s], round_of(s, turn, half) + (USED[s] + 1))
                    for h in range(2):
                        nc.scalar.copy(yrow[:, h, :], ps[6 + h][:, :]).then_inc(S["y_copied"], 1)
                    act.wait_ge(S["wpT_ready"], it + 1)
                    nc.scalar.copy(wpT, ps[5][:, 0:NT]).then_inc(S["wpT_done"], 1)
            def squares(name, first):
                for i, (t0, n) in enumerate(TOK):
                    act.wait_ge(S[name], first + (2 * i if name == "added" else 0))
                    if name != "added":
                        act.wait_ge(S["ss2"], 6)
                    if i:
                        act.wait_ge(S["ss2" if name == "added" else "ov_ss"], (3 if name == "added" else 0) + i)
                    ac(junk_x[0:n, :], h2[0:n, i, :], ACT.Square, accum_out=ss[0:n, i:i + 1]).then_inc(
                        S["ss2" if name == "added" else "ov_ss"], 1)

            squares("added", 6 * (NE // 2) + 2)
            act.wait_ge(S["slots"], 1)
            n_ov = act.value_load(ovi[0:1, 15:16], min_val=0, max_val=OV)
            with act.If(n_ov > 0):
                with act.Fori(0, n_ov) as j:
                    act.wait_ge(S["ov_g"], j + 1)
                    ac(sil[0:CAP, :], ps[2][0:CAP, :], ACT.Silu).then_inc(S["ov_sil"], 1)
                    act.wait_ge(S["ov_wT"], j + 1)
                    nc.scalar.copy(wpT, ps[5][:, 0:NT]).then_inc(S["ov_wpT"], 1)
                    act.wait_ge(S["ov_t"], j + 1)
                    nc.scalar.copy(hidT[:, :, 0:CAP], ps[4][:, :].rearrange("p (k s) -> p k s", k=KE)[:, :, 0:CAP]).then_inc(
                        S["ov_hidT"], 1)
                    act.wait_ge(S["ov_dn"], j + 2)
                    for h in range(2):
                        nc.scalar.copy(yrow[0:CAP, h, :], ps[6 + h][0:CAP, :]).then_inc(S["ov_y"], 1)
                squares("fin_sum", 1)

        @block.gpsimd
        def _(pool):
            gp = nc.gpsimd
            cnt = [0]

            def link(ins):
                cnt[0] += 1
                ins.then_inc(S["pool"], 1)
                pool.wait_ge(S["pool"], cnt[0])

            gp.memset(epsc[:, :], EPS)
            gp.memset(ss[:, :], 1.0)
            link(gp.memset(ident[:, :], 0.0))
            link(gp.affine_select(out=ident[:, :], in_=ident[:, :], compare_op=ALU.not_equal, fill=1.0, base=0,
                                  pattern=[[-1, P]], channel_multiplier=1))
            pool.sem_inc(S["consts"], 1)
            link(gp.memset(ones[:, :], 1.0))
            gp.memset(cmask[:, :], 1.0)
            link(gp.memset(smask[:, :], 1.0))
            for c in range(NCH):
                gp.memset(cmask[:, CH * c:CH * c + 1], 0.0)
            gp.memset(smask[:, 0:1], 0.0)
            gp.memset(cmask[:, NP_TOK:NT:SEQ_S], 0.0)
            link(gp.memset(smask[:, NP_TOK:NT:SEQ_S], 0.0))
            link(gp.memset(seqm[:, :], 1.0))
            link(gp.affine_select(out=seqm[:, :], in_=seqm[:, :], compare_op=ALU.is_ge, fill=0.0, base=0,
                                  pattern=[[-SEQ_S, NB]], channel_multiplier=1))
            link(gp.affine_select(out=seqm[:, :], in_=seqm[:, :], compare_op=ALU.is_ge, fill=0.0, base=SEQ_S - 1,
                                  pattern=[[SEQ_S, NB]], channel_multiplier=-1))
            gp.iota(par_i[:, 0:1], pattern=[[0, 1]], base=0, channel_multiplier=1)
            link(gp.iota(iota_i[:, :], pattern=[[1, P]], base=0, channel_multiplier=0))
            link(gp.tensor_copy(iota_s[:, :], iota_i[:, :]))
            link(gp.iota(iota_i[:, 0:NE], pattern=[[-1, NE]], base=NE, channel_multiplier=0))
            link(gp.tensor_copy(rev[:, :], iota_i[:, 0:NE]))
            link(gp.memset(bd[:, :, :, :, :].rearrange("p r t q c -> p (r t q c)"), 0.0))
            pool.sem_inc(S["consts"], 1)

            def level(q, n):
                t0, m = T5Q * q, 2 ** n
                half = slice(T5Q * (q % 2), T5Q * (q % 2 + 1))
                co, si = cosT[:, half, :], sinT[:, half, :]
                if n == 0:
                    link(gp.memset(co[:, :, 0:1], 1.0))
                    link(gp.memset(si[:, :, 0:1], 0.0))
                if q == 0 and n > 0:
                    c, s, c2, s2 = pw[:, n - 1, 0, :], pw[:, n - 1, 1, :], pw[:, n, 0, :], pw[:, n, 1, :]
                    link(gp.tensor_tensor(cf[:, 16, :], c, c, ALU.mult))
                    link(gp.tensor_tensor(cf[:, 17, :], s, s, ALU.mult))
                    link(gp.tensor_tensor(cf[:, 18, :], c, s, ALU.mult))
                    link(gp.tensor_tensor(c2, cf[:, 16, :], cf[:, 17, :], ALU.subtract))
                    link(gp.tensor_tensor(s2, cf[:, 18, :], cf[:, 18, :], ALU.add))
                pc, psn = bt(pw[:, n, 0, t0:t0 + T5Q], m), bt(pw[:, n, 1, t0:t0 + T5Q], m)
                tv = ptab[:, 0:T5Q * m].rearrange("p (t n) -> p t n", t=T5Q)
                link(gp.tensor_tensor(co[:, :, m:2 * m], co[:, :, 0:m], pc, ALU.mult))
                link(gp.tensor_tensor(tv, si[:, :, 0:m], psn, ALU.mult))
                link(gp.tensor_tensor(co[:, :, m:2 * m], co[:, :, m:2 * m], tv, ALU.subtract))
                link(gp.tensor_tensor(si[:, :, m:2 * m], si[:, :, 0:m], pc, ALU.mult))
                link(gp.tensor_tensor(tv, co[:, :, 0:m], psn, ALU.mult))
                link(gp.tensor_tensor(si[:, :, m:2 * m], si[:, :, m:2 * m], tv, ALU.add))
                if n == LEVELS - 1:
                    for v in (co, si):
                        link(gp.tensor_copy(v[:, :, NP_TOK:NT].rearrange("p t (b s) -> p t b s", s=SEQ_S),
                                            v[:, :, 0:SEQ_S].unsqueeze(2).broadcast_to([P, T5Q, NB, SEQ_S])))
                    pool.sem_inc(S["tab_done"], 1)

            pool.wait_ge(S["phasor"], 1)
            for n in range(LEVELS):
                level(0, n)
            for st in STEPS:
                kind = st[0]
                if kind == "sc":
                    _, g, i = st
                    pool.wait_ge(S["sc_raw"], 3 * g + i + 1)
                    if i < 2:
                        link(gp.affine_select(out=scp[:, i], in_=scp[:, i], compare_op=ALU.is_ge, fill=0.0, base=0,
                                              pattern=[[0, GH], [1, P]], channel_multiplier=-1))
                        link(gp.memset(scp[0:CH, i, :, CH:P], 0.0))
                        pool.sem_inc(S["sc_done"], 1)
                    else:
                        link(gp.affine_select(out=scs[:, :, :], in_=scs[:, :, :], compare_op=ALU.is_ge, fill=0.0, base=0,
                                              pattern=[[0, GH], [1, NS_TOK]], channel_multiplier=-1))
                        v = scs[:, :, :].rearrange("p h (b s) -> p h b s", s=SEQ_S)
                        link(gp.affine_select(out=v, in_=v, compare_op=ALU.is_ge, fill=0.0, base=0,
                                              pattern=[[0, GH], [-SEQ_S, NB], [0, SEQ_S]], channel_multiplier=1))
                        pool.sem_inc(S["sc_done"], 1)
                elif kind == "bu":
                    t = st[1]
                    s, tt = t % 2, t % (2 * T5Q)
                    pool.wait_ge(S["g_done"], 2 * t + 2)
                    if t >= 2:
                        pool.wait_ge(S["h_used"], t - 1)
                        pool.wait_ge(S["fs_done"], t - 1)
                    link(gp.tensor_tensor(pt1, gr[:, s, :], sinT[:, tt, :], ALU.mult))
                    link(gp.tensor_tensor(pt2, gi[:, s, :], cosT[:, tt, :], ALU.mult))
                    gp.tensor_tensor(hi[:, s, :], pt1, pt2, ALU.add).then_inc(S["h_done"], 1)
                    pool.wait_ge(S["h_done"], t + 1)
                    if t < T5 - T5Q:
                        for n in ((0, 1, 2), (3, 4, 5), (6, 7), ())[t % T5Q]:
                            level(t // T5Q + 1, n)
            pool.wait_ge(S["h_used"], T5)
            pool.wait_ge(S["fs_done"], T5)
            link(gp.affine_select(out=upper, in_=ones[:, :], compare_op=ALU.is_gt, fill=0.0, base=0,
                                  pattern=[[1, P]], channel_multiplier=-1))
            pool.sem_inc(S["upper_done"], 1)
            wait_filled(pool, ("rank",))
            gp.memset(wpT, 0.0)
            link(gp.memset(yrow[:, :, :], 0.0))
            pool.sem_inc(S["no_rows"], 1)

        @block.vector
        def _(dve):
            v_ = nc.vector
            cnt, name = [0], ["dve"]

            def link(ins):
                cnt[0] += 1
                ins.then_inc(S[name[0]], 1)
                dve.wait_ge(S[name[0]], cnt[0])

            TT, TS, STT = v_.tensor_tensor, v_.tensor_scalar, v_.scalar_tensor_tensor

            def rsqrt_rows(i, n, tiles=1):
                ms, y, w = (rs[0:n, c, i:i + tiles] for c in range(3))
                link(TS(ms, ss[0:n, i:i + tiles], 1.0 / D, EPS, ALU.mult, ALU.add))
                link(TS(w.bitcast(I32), ms.bitcast(I32), 1, None, ALU.logical_shift_right))
                link(TS(y.bitcast(I32), w.bitcast(I32), -1.0, float(0x5f3759df), ALU.mult, ALU.add))
                for _ in range(3):
                    link(TT(w, y, y, ALU.mult))
                    link(TT(w, w, ms, ALU.mult))
                    link(TS(w, w, -0.5, 1.5, ALU.mult, ALU.add))
                    link(TT(y, y, w, ALU.mult))
                return y

            for i, (t0, n) in enumerate(TOK):
                dve.wait_ge(S["ss_done"], i + 1)
                y = rsqrt_rows(i, n)
                dve.wait_ge(gmix_in, 16)
                if i == 2:
                    dve.wait_ge(filled[BANK[("xt", 0, 1)][0]], BANK[("xt", 0, 1)][1] + 1)
                STT(xn[0:n, i % 2, :], h2[0:n, i, :], y, grow[0:n, :], ALU.mult, ALU.mult).then_inc(S["xn_done"], 1)
            C = lambda i: cf[:, i, :]
            lre, lim = pcol[:, 44:60], pcol[:, 60:76]

            def params():
                st = ("params",)
                wait_filled(dve, st)
                is_emptied(v_.tensor_copy(pcol[:, :], bank(st, 76)), st)
                dve.wait_ge(emptied[BANK[st][0]], BANK[st][1] + 1)
                dve.wait_ge(S["dt_exp"], 2)
                link(TT(C(1), lre, C(0), ALU.mult))
                dve.sem_inc(S["mag_in"], 1)
                r0, r1_ = pcol[:, 0:8], pcol[:, 8:16]
                link(TT(lb[:, 2, :], r0, r1_, ALU.max))
                TT(lb[:, 0, :], r0, lb[:, 2, :], ALU.subtract)
                link(TT(lb[:, 1, :], r1_, lb[:, 2, :], ALU.subtract))
                dve.sem_inc(S["lb_in"], 1)
                link(TT(C(2), lim, C(0), ALU.mult))
                link(TS(C(4), C(2), 1.0 / (2 * np.pi), 12582912.0, ALU.mult, ALU.add))
                link(TS(C(4), C(4), -12582912.0, None, ALU.add))
                two_pi = 2 * np.pi
                c1 = 6.28125
                c2 = float(np.float32(np.floor((two_pi - c1) * 2 ** 21) / 2 ** 21))
                c3 = two_pi - c1 - c2
                for c in (c1, c2, c3):
                    link(STT(C(2), C(4), -c, C(2), ALU.mult, ALU.add))
                link(TS(C(2), C(2), 0.25, None, ALU.mult))
                link(TT(C(7), C(2), C(2), ALU.mult))
                link(TS(C(8), C(7), 1.0 / 362880, -1.0 / 5040, ALU.mult, ALU.add))
                for c in (1.0 / 120, -1.0 / 6, 1.0):
                    link(TT(C(8), C(8), C(7), ALU.mult))
                    link(TS(C(8), C(8), c, None, ALU.add))
                link(TT(C(6), C(8), C(2), ALU.mult))
                link(TS(C(8), C(7), -1.0 / 3628800, 1.0 / 40320, ALU.mult, ALU.add))
                for c in (-1.0 / 720, 1.0 / 24, -0.5, 1.0):
                    link(TT(C(8), C(8), C(7), ALU.mult))
                    link(TS(C(8), C(8), c, None, ALU.add))
                link(v_.tensor_copy(C(5), C(8)))
                for _ in range(2):
                    link(TT(C(8), C(5), C(6), ALU.mult))
                    link(TT(C(9), C(6), C(6), ALU.mult))
                    link(TS(C(6), C(8), 2.0, None, ALU.mult))
                    link(TS(C(5), C(9), -2.0, 1.0, ALU.mult, ALU.add))
                v_.tensor_copy(pw[:, 0, 0, :], C(5))
                link(v_.tensor_copy(pw[:, 0, 1, :], C(6)))
                dve.sem_inc(S["phasor"], 1)
                dve.wait_ge(S["mag_exp"], 1)
                TT(C(10), C(3), C(5), ALU.mult)
                TT(C(11), C(3), C(6), ALU.mult)
                link(TT(C(12), lre, lre, ALU.mult))
                link(TT(C(13), lim, lim, ALU.mult))
                link(TT(C(12), C(12), C(13), ALU.add))
                link(v_.reciprocal(C(12), C(12)))
                link(TS(C(13), C(10), -1.0, None, ALU.add))
                TT(C(14), C(13), lre, ALU.mult)
                link(TT(C(15), C(11), lim, ALU.mult))
                link(TT(C(14), C(14), C(15), ALU.add))
                TT(C(15), C(11), lre, ALU.mult)
                link(TT(C(13), C(13), lim, ALU.mult))
                link(TT(C(15), C(15), C(13), ALU.subtract))
                TT(C(14), C(14), C(12), ALU.mult)
                link(TT(C(15), C(15), C(12), ALU.mult))
                dve.wait_ge(S["consts"], 2)
                cr, ci = bt(C(14), CG), bt(C(15), CG)
                for r in range(2):
                    TT(ptmp, braw[:, r], cr, ALU.mult)
                    link(TT(ptmp2, braw[:, 1 - r], ci, ALU.mult))
                    for q in range(2):
                        h = slice(ST * q, ST * (q + 1))
                        last = TT(bd[h, r, :, q, :], ptmp[h], ptmp2[h], ALU.add if r else ALU.subtract)
                    link(last)
                    dve.sem_inc(S["bdcd"], 1)
                link(TS(par_i[:, 1:2], par_i[:, 0:1], 4, 1, ALU.logical_shift_right, ALU.bitwise_and))
                link(v_.tensor_copy(par[:, 1:2], par_i[:, 1:2]))
                link(TS(par[:, 0:1], par[:, 1:2], -1.0, 1.0, ALU.mult, ALU.add))
                link(TS(negp[:, :], par[:, :], -1.0, None, ALU.mult))
                for r in range(2):
                    for q in range(2):
                        last = TS(cd[:, r, :, q, :], craw[:, r], (negp if r else par)[:, q:q + 1], None, ALU.mult)
                    link(last)
                    dve.sem_inc(S["bdcd"], 1)
                dve.wait_ge(S["lb_exp"], 1)
                link(TT(lb[:, 2, :], lb[:, 0, :], lb[:, 1, :], ALU.add))
                link(v_.reciprocal(lb[:, 2, :], lb[:, 2, :]))
                link(TT(lb[:, 0, :], lb[:, 0, :], lb[:, 2, :], ALU.mult))
                link(TS(lb[:, OML, :], lb[:, 0, :], -1.0, 1.0, ALU.mult, ALU.add))
                link(TS(lb[:, NOML, :], lb[:, OML, :], -1.0, None, ALU.mult))
                dve.sem_inc(S["lb_done"], 1)

            for st in STEPS:
                kind = st[0]
                if kind == "params":
                    params()
                elif kind == "h0":
                    wait_filled(dve, st)
                    is_emptied(v_.tensor_copy(arena[:, int(113.5 * K):int(113.5 * K) + 2 * P], bank(st, 2 * P)), st)
                    dve.wait_ge(emptied[BANK[st][0]], BANK[st][1] + 1)
                    for r in range(2):
                        hv = ptmp.rearrange("p t c -> p (t c)")[:, 0:P].rearrange("p (t b) -> p t b", b=NB)
                        TT(ah[:, r], h0t[:, r], bt(C(10), NB), ALU.mult)
                        link(TT(hv, h0t[:, 1 - r], bt(C(11), NB), ALU.mult))
                        link(TT(ah[:, r], ah[:, r], hv, ALU.add if r else ALU.subtract))
                elif kind in ("bt", "ct"):
                    wait_filled(dve, st)
                    dst = (btr if kind == "bt" else ctr)[:, st[1]].rearrange("p t n -> p (t n)")
                    link(v_.tensor_copy(dst, bank(st)))
                    dve.sem_inc(emptied[BANK[st][0]], 1)
                    dve.sem_inc(S["bdcd"], 1)
                elif kind == "proj":
                    _, u, j = st
                    if u[0] == "q":
                        g = int(u[1])
                        wait_filled(dve, st)
                        TS(oT[:, GH + j, :] if g else qd[:, j, :], bank(st, NT), HG_SCALE, None, ALU.mult).then_inc(S["q_done"], 1)
                        dve.wait_ge(S["q_done"], GH * g + j + 1)
                        dve.sem_inc(emptied[BANK[st][0]], 1)
                    elif u == "za":
                        wait_filled(dve, st)
                        dve.wait_ge(S["sig_g"], j + 1)
                        STT(sga[:, j % 2, :], bank(st, NT), pcol[:, 24 + j:25 + j], sga[:, j % 2, :], ALU.add,
                            ALU.mult).then_inc(S["y_b"], 1)
                        dve.wait_ge(S["y_b"], j + 1)
                        dve.sem_inc(emptied[BANK[st][0]], 1)
                        dve.wait_ge(S["sig_b"], j + 1)
                        TT(merged[:, j, :], merged[:, j, :], sga[:, j % 2, :], ALU.mult).then_inc(S["yb_done"], 1)
                    elif u[0:2] == "wa":
                        m = 4 * int(u[2]) + j
                        wait_filled(dve, st)
                        dve.wait_ge(S["sig_a"], m + 1)
                        TT(sga[:, m % 2, :], bank(st, NT), sga[:, m % 2, :], ALU.mult).then_inc(S["y_a"], 1)
                        dve.wait_ge(S["y_a"], m + 1)
                        dve.sem_inc(emptied[BANK[st][0]], 1)
                        dve.wait_ge(S["yb_done"], m + 1)
                        TT(merged[:, m, :], merged[:, m, :], sga[:, m % 2, :], ALU.add).then_inc(S["merged_ok"], 1)
                elif kind == "gate":
                    hh = st[1]
                    dve.wait_ge(S["sil_o"], hh + 1)
                    dve.wait_ge(S["on_done"], hh + 1)
                    STT(oT[:, hh, :], oT[:, hh, :], pcol[:, 16 + hh:17 + hh], sgo[:, hh % 2, :], ALU.mult,
                        ALU.mult).then_inc(S["o_final"], 1)
                elif kind == "log":
                    g = st[1]
                    dve.wait_ge(S["logf"], GH * (g + 1))
                    for h in range(GH):
                        hh = GH * g + h
                        TS(kk[:, h, :], kk[:, h, :], lb[:, NOML, hh:hh + 1], lb[:, OML, hh:hh + 1], ALU.mult,
                           ALU.add).then_inc(S["k_done"], 1)
                    for h in range(GH):
                        v_.tensor_tensor_scan(bc[:, h, :], cmask[:, :], bc[:, h, :], 0.0, ALU.mult, ALU.add).then_inc(
                            S["scan_done"], 1)
                elif kind == "exp":
                    g = st[1]
                    dve.wait_ge(S["exp_done"], 2 * g + 2)
                    if g:
                        dve.wait_ge(S["st_sum"], 2 * GH)
                    v_.tensor_copy(blast[:, :, 0:NCH], bc[:, :, CH - 1:NP_TOK:CH])
                    v_.tensor_copy(blast[:, :, NCH:], bc[:, :, NP_TOK + SEQ_S - 1:NT:SEQ_S])
                    v_.tensor_copy(eblast[:, :, 0:NCH], eb[:, :, CH - 1:NP_TOK:CH])
                    link(v_.tensor_copy(eblast[:, :, NCH:], eb[:, :, NP_TOK + SEQ_S - 1:NT:SEQ_S]))
                    for h in range(GH):
                        for (c0, c1, n, lo) in ((0, NCH, CH, 0), (NCH, 12, SEQ_S, NP_TOK)):
                            v = bc[:, h, lo:lo + (c1 - c0) * n].rearrange("p (c s) -> p c s", s=n)
                            last = TT(v, bt(blast[:, h, c0:c1], n), v, ALU.subtract)
                    last.then_inc(S["diff_done"], 1)
                    dve.wait_ge(S["q_done"], GH * (g + 1))
                    if g:
                        wait_filled(dve, ("o", 0, GH - 1))
                    TT(qd[:, :, :], oT[:, GH:, :] if g else qd[:, :, :], eb[:, :, :], ALU.mult).then_inc(S["qd_done"], 1)
                    dve.wait_ge(S["k_done"], GH * (g + 1))
                    TT(kd[:, :, :], kd[:, :, :], kk[:, :, :], ALU.mult).then_inc(S["kd_done"], 1)
                elif kind == "decay":
                    g = st[1]
                    dve.wait_ge(S["dexp"], g + 1)
                    TT(bc[:, :, :], bc[:, :, :], kk[:, :, :], ALU.mult).then_inc(S["kl_done"], 1)
                elif kind == "ds":
                    _, g, c = st
                    wait_filled(dve, st)
                    if g and c == 0:
                        dve.wait_ge(S["out_done"], 16)
                        dve.wait_ge(filled[BANK[("o", 0, GH - 1)][0]], BANK[("o", 0, GH - 1)][1] + 1)
                    for h in range(GH):
                        cs = slice(h * P, (h + 1) * P)
                        if c == 0:
                            last = v_.tensor_copy(sp_[:, 0, cs], bank(st)[:, cs])
                        else:
                            last = STT(sp_[:, c, cs], sp_[:, c - 1, cs], eblast[:, h, c:c + 1], bank(st)[:, cs], ALU.mult,
                                       ALU.add)
                    last.then_inc(S["state_new"], 1)
                    dve.wait_ge(S["state_new"], NCH * g + c + 1)
                    dve.sem_inc(emptied[BANK[st][0]], 1)
                elif kind == "o":
                    _, g, h = st
                    hh = GH * g + h
                    dve.wait_ge(S["v_done"], 3 * (g + 1))
                    if hh:
                        wait_filled(dve, ("dss", (hh - 1) // GH, (hh - 1) % GH, 1))
                    TT(vm[:, :, :], vn[0:NS_TOK, 2, h * P:(h + 1) * P].unsqueeze(1).broadcast_to([NS_TOK, NB, P]),
                       bt(seqm[:, :], P), ALU.mult).then_inc(S["vm_done"], 1)
                elif kind == "dss":
                    _, g, h, i = st
                    hh = GH * g + h
                    wait_filled(dve, st)
                    dve.wait_ge(st_in[h], 16 * (g + 1))
                    wait_filled(dve, ("o", g, h))
                    for b in range(4 * i, 4 * i + 4):
                        last = STT(stt_[h][:, b, :], stt_[h][:, b, :], eblast[:, h, NCH + b:NCH + b + 1],
                                   bank(st)[:, (b % 4) * P:(b % 4 + 1) * P], ALU.mult, ALU.add)
                    last.then_inc(S["st_sum"], 1)
                    dve.wait_ge(S["st_sum"], 2 * hh + i + 1)
                    dve.sem_inc(emptied[BANK[st][0]], 1)
                elif kind == "mean":
                    _, g, h = st
                    hh = GH * g + h
                    dve.wait_ge(S["rstd_done"], hh + 1)
                    TT(oT[:, hh, :], oT[:, hh, :], rstd_o, ALU.mult).then_inc(S["on_done"], 1)
                elif kind == "bu":
                    t = st[1]
                    s, tt = t % 2, t % (2 * T5Q)
                    if t % T5Q == 0:
                        dve.wait_ge(S["tab_done"], t // T5Q + 1)
                    Ct, Sn = cosT[:, tt, :], sinT[:, tt, :]
                    wait_filled(dve, ("bur", t))
                    wait_filled(dve, ("bui", t))
                    br, bi = bank(("bur", t), NT), bank(("bui", t), NT)
                    if t:
                        dve.wait_ge(S["g_done"], 2 * t)
                        dve.wait_ge(S["hr_done"], t)
                    TT(wr, br, Ct, ALU.mult)
                    TT(tm1, bi, Sn, ALU.mult)
                    TT(wi, bi, Ct, ALU.mult)
                    link(TT(tm2, br, Sn, ALU.mult))
                    dve.sem_inc(emptied[2], 1)
                    dve.sem_inc(emptied[3], 1)
                    TT(wr, wr, tm1, ALU.add)
                    TT(wi, wi, tm2, ALU.subtract)
                    link(TS(rdec, smask[:, :], cf[:, 3, t:t + 1], None, ALU.mult))
                    TT(wr[:, NP_TOK:NT:SEQ_S], wr[:, NP_TOK:NT:SEQ_S], ah[:, 0, t, :], ALU.add)
                    link(TT(wi[:, NP_TOK:NT:SEQ_S], wi[:, NP_TOK:NT:SEQ_S], ah[:, 1, t, :], ALU.add))
                    if t >= 2:
                        dve.wait_ge(S["h_done"], t - 1)
                    v_.tensor_tensor_scan(gr[:, s, :], rdec, wr, 0.0, ALU.mult, ALU.add).then_inc(S["g_done"], 1)
                    v_.tensor_tensor_scan(gi[:, s, :], rdec, wi, 0.0, ALU.mult, ALU.add).then_inc(S["g_done"], 1)
                    dve.wait_ge(S["g_done"], 2 * t + 2)
                    TT(tm1, gr[:, s, :], Ct, ALU.mult)
                    link(TT(tm2, gi[:, s, :], Sn, ALU.mult))
                    if t >= 2:
                        dve.wait_ge(S["h_used"], t - 1)
                        dve.wait_ge(S["fs_done"], t - 1)
                    TT(hr[:, s, :], tm1, tm2, ALU.subtract).then_inc(S["hr_done"], 1)
                elif kind == "sy":
                    t = st[1]
                    s = t % 2
                    dve.wait_ge(S["h_done"], t + 1)
                    dve.wait_ge(S["hr_done"], t + 1)
                    for r, hv in enumerate((hr, hi)):
                        v_.tensor_copy(fsp[:, r, t:t + 1], hv[:, s, NP_TOK - 1:NP_TOK])
                        last = v_.tensor_copy(fss[:, r, :, t], hv[:, s, NP_TOK + SEQ_S - 1:NT:SEQ_S])
                    last.then_inc(S["fs_done"], 1)
                    if t % 4 == 3:
                        T = t // 4
                        dve.wait_ge(S["h_used"], t + 1)
                        STT(gy[:, T, :], uT[:, T, :], pcol[:, 40 + T:41 + T], ps[4][:, 0:NT], ALU.mult, ALU.add).then_inc(
                            S["y5_ev"], 1)
                        dve.wait_ge(S["y5_ev"], T + 1)
                        dve.sem_inc(emptied[4], 1)
                elif kind == "mix":
                    _, i, h = st
                    n = TOK[i][1]
                    if (i, h) != (2, 1):
                        wait_filled(dve, st)
                        for c in (h,) if n == P else (0, 1):
                            hv = h2[0:n, i, 512 * c:512 * (c + 1)]
                            r = 0 if n == P else n * c
                            TT(hv, bank(st)[r:r + n, :], hv, ALU.add).then_inc(S["h2_done"], 1)
                        dve.wait_ge(S["h2_done"], 2 * i + (h + 1 if n == P else 2))
                        dve.sem_inc(emptied[BANK[st][0]], 1)
                    if h == 1:
                        dve.wait_ge(late_in, 9 * 16)
                        dve.wait_ge(S["ss2"], i + 1)
                        y = rsqrt_rows(i, n)
                        by_p = lambda v: v.rearrange("p (c k) -> p c k", k=KD)
                        STT(hn[0:n, i, :].rearrange("p (k c) -> p c k", k=KD), by_p(h2[0:n, i, :]), y,
                            by_p(gffn[0:n, :]), ALU.mult, ALU.mult).then_inc(
                            S["hn_done"], 1)
                elif kind == "logits":
                    i = st[1]
                    n = TOK[i][1]
                    if i == 0:
                        link(v_.memset(lg[:, :, :], 0.0))
                    wait_filled(dve, st)
                    link(TT(lg[0:n, i, :], bank(st, NG + NE, n), brt[0:n, :], ALU.add))
                    dve.sem_inc(emptied[BANK[st][0]], 1)

            RED = v_.tensor_reduce
            gl = lg[:, :, 0:NG]
            el = lg[:, :, NG:].rearrange("p t (g e) -> p t g e", g=NG)
            A1, A2, M = r32[0], r32[1], r32[2]
            rv4 = rev[:, NE - NG:].unsqueeze(1).broadcast_to([P, 3, NG])
            rv8 = rev[:, NE - NE_G:].unsqueeze(1).broadcast_to([P, 3, NE_G])
            gx = r32[3][:, :, 0, 0:NG]
            link(RED(r1[0], gl, X, ALU.max))
            link(TT(gx, gl, r1[0].broadcast_to([P, 3, NG]), ALU.subtract))
            e4 = r8[0][:, :, 0:NG]
            og = r8[1][:, :, 0:NG]
            link(TS(e4, gx, 0.0, None, ALU.is_equal))
            link(TT(e4, e4, rv4, ALU.mult))
            link(RED(r1[1], e4, X, ALU.max))
            link(TT(og, rv4, r1[1].broadcast_to([P, 3, NG]), ALU.is_equal))
            link(TT(r32[4], el, bt(og, NE_G), ALU.mult))
            es = r8[2]
            link(RED(es, r32[4].rearrange("p t g e -> p t e g"), X, ALU.add))
            oh = []
            for k in range(2):
                vmax = r1[2 + k]
                link(RED(vmax, es, X, ALU.max))
                link(TT(r8[3], es, vmax.broadcast_to([P, 3, NE_G]), ALU.is_equal))
                link(TT(r8[3], r8[3], rv8, ALU.mult))
                link(RED(r1[4], r8[3], X, ALU.max))
                link(TT(r8[4 + k], rv8, r1[4].broadcast_to([P, 3, NE_G]), ALU.is_equal))
                oh.append(r8[4 + k])
                if k == 0:
                    link(STT(es, r8[4], -BIG, es, ALU.mult, ALU.add))
            link(TT(r1[8], r1[3], r1[2], ALU.subtract))
            for k, A in enumerate((A1, A2)):
                link(TT(A, bt(og, NE_G), oh[k].unsqueeze(2).broadcast_to([P, 3, NG, NE_G]), ALU.mult))
                link(v_.memset(A[NS_TOK:P, 2, :, :], 0.0))
            link(TT(M, A1, A2, ALU.add))
            dve.sem_inc(S["mats"], 1)
            dve.sem_inc(S["gexp_in"], 1)
            dve.wait_ge(S["gexp"], 2)
            link(RED(r1[5], gx, X, ALU.add))
            link(TS(r1[6], r1[8], 1.0, None, ALU.add))
            link(TT(r1[5], r1[5], r1[6], ALU.mult))
            link(v_.reciprocal(r1[5], r1[5]))
            link(v_.tensor_copy(wtop[:, 0, :].unsqueeze(2), r1[5]))
            link(TT(wtop[:, 1, :].unsqueeze(2), r1[5], r1[8], ALU.mult))
            st = ("rank",)
            wait_filled(dve, st)
            rk = r32[5]
            link(v_.tensor_copy(rk.rearrange("p t g e -> p (t g e)"), bank(st, 3 * NE)))
            link(v_.tensor_copy(nE, ps[BANK[st][0]][:, 3 * NE:4 * NE]))
            dve.sem_inc(emptied[BANK[st][0]], 1)
            link(TS(ovt, nE, float(CAP), None, ALU.is_gt))
            for k in range(2, (NT + CAP - 1) // CAP):
                link(STT(ovt, nE, float(CAP * k), ovt, ALU.is_gt, ALU.add))
            link(v_.tensor_tensor_scan(incl, ones[:, 0:NE], ovt, 0.0, ALU.mult, ALU.add))
            link(TT(corr, incl, ovt, ALU.subtract))
            link(TT(corr, corr, rev[:, :], ALU.add))
            link(TS(corr, corr, -1.0, float(CAP), ALU.add, ALU.mult))
            flat = lambda v: v.rearrange("p t g e -> p t (g e)")
            b3 = lambda v: v.unsqueeze(1).broadcast_to([P, 3, NE])
            link(TS(r32[6], rk, float(CAP), None, ALU.is_ge))
            link(TT(flat(r32[6]), flat(r32[6]), b3(corr), ALU.mult))
            link(TT(r32[6], r32[6], rk, ALU.add))
            link(TS(r32[7].rearrange("p t g e -> p (t g e)")[:, 0:NE], iota_s[:, 0:NE], float(CAP), None,
                                  ALU.mult))
            link(TT(flat(r32[6]), flat(r32[6]), b3(r32[7].rearrange("p t g e -> p (t g e)")[:, 0:NE]), ALU.add))
            for k, A in enumerate((A1, A2)):
                link(TT(r32[3], A, r32[6], ALU.mult))
                link(RED(slot[:, k, :].unsqueeze(2), flat(r32[3]), X, ALU.add))
                link(v_.memset(slot[NS_TOK:P, k, 2:3], -1.0e9))
            link(v_.tensor_copy(wslot[:, :, :], slot[:, :, :]))
            def build(width, first, shifted, done, picked):
                for i in range(3):
                    last = TS(pick[:, i, 0:width], iota_s[:, 0:width], slot[:, 0, i:i + 1], None, ALU.is_equal)
                last.then_inc(S["dve"], 1)
                dve.wait_ge(S["dve"], first)
                for i in range(3):
                    last = STT(pick[:, i, 0:width], iota_s[:, 0:width], slot[:, 1, i:i + 1], pick[:, i, 0:width],
                               ALU.is_equal, ALU.add)
                last.then_inc(S[done], 1)
                dve.wait_ge(S[done], picked)
                TS(slot[:, :, :], slot[:, :, :], -float(width), None, ALU.add).then_inc(S["dve"], 1)
                dve.wait_ge(S["dve"], shifted)

            def build_weighted(width, first, shifted, done, picked):
                for k, dst in enumerate((wpick, wtmp)):
                    for i in range(3):
                        last = TS(dst[:, i, 0:width], iota_s[:, 0:width], wslot[:, k, i:i + 1], wtop[:, k, i:i + 1],
                                  ALU.is_equal, ALU.mult)
                last.then_inc(S["dve"], 1)
                dve.wait_ge(S["dve"], first)
                v = wpick[:, :, 0:width]
                TT(v, v, wtmp[:, :, 0:width], ALU.add).then_inc(S[done], 1)
                dve.wait_ge(S[done], picked)
                TS(wslot[:, :, :], wslot[:, :, :], -float(width), None, ALU.add).then_inc(S["dve"], 1)
                dve.wait_ge(S["dve"], shifted)

            def add_share(c, name):
                t0, n = TOK[c // 2]
                b, r = SHARE[c]
                hv = h2[0:n, c // 2, 512 * (c % 2):512 * (c % 2 + 1)]
                TT(hv, ps[b][r:r + n, :], hv, ALU.add).then_inc(S[name], 1)

            def copy_xT(width):
                for b in range(2):
                    last = v_.tensor_copy(xT[:, 4 * b:4 * b + 4, 0:width],
                                          ps[b][:, :].rearrange("p (k s) -> p k s", k=4)[:, :, 0:width])
                return last

            build(P, cnt[0] + 1, cnt[0] + 2, "pick_done", 1)
            cnt[0] += 2
            tiles = r8[6].rearrange("p t e -> p (t e)")[:, 0:OV]
            link(TT(ovj, incl.unsqueeze(1).broadcast_to([P, OV, NE]), bt(iota_s[:, 0:OV], NE), ALU.is_le))
            link(RED(tiles.unsqueeze(2), ovj, X, ALU.add))
            link(TS(tiles, tiles, float(NE - 1), None, ALU.min))
            link(v_.tensor_copy(ovi[:, 0:OV], tiles))
            link(v_.tensor_copy(ovi[:, 15:16], incl[:, NE - 1:NE]))
            dve.sem_inc(S["slots"], 1)
            dve.sem_inc(S["hid_done"], 1)
            b0 = cnt[0]
            in_order = lambda v, rows: v[0:rows, :].rearrange("p (c k) -> p k c", k=KE)
            with dve.Fori(0, NE // 4) as turn:
                for half in range(2):
                    it = turn * 2 + half
                    def add_shares():
                        for c in range(6):
                            dve.wait_ge(S["shared"], it * 6 + SHARED[c])
                            add_share(c, "added")
                        dve.wait_ge(S["added"], it * 6 + 6)

                    if half == 0:
                        dve.wait_ge(S["sel_done"], it + 1)
                        copy_xT(P).then_inc(S["xT_done"], 1)
                    build(P, it * 4 + (b0 + 1), it * 4 + (b0 + 2), "pick_done", it + 2)
                    if half == 1:
                        add_shares()
                    for s in UP_SLOT:
                        dve.wait_ge(used[s], round_of(s, turn, half) + (USED[s] + 1))
                    dve.wait_ge(S["silu_done"], it + 1)
                    TT(hid[:, :].rearrange("p (k c) -> p k c", k=KE), in_order(ps[3], P), in_order(sil, P),
                       ALU.mult).then_inc(S["hid_done"], 1)
                    build_weighted(P, it * 4 + (b0 + 3), it * 4 + (b0 + 4), "wpick_done", it + 1)
                    if half == 0:
                        dve.wait_ge(S["sel_done"], it + 2)
                        copy_xT(P).then_inc(S["xT_done"], 1)
                        add_shares()
            for c in range(6):
                dve.wait_ge(S["shared"], 6 * (NE // 2) + SHARED[c])
                add_share(c, "added")
            dve.wait_ge(S["added"], 6 * (NE // 2 + 1))
            b1 = b0 + 2 * NE + 1
            TS(slot[:, :, :], slot[:, :, :], float(P), None, ALU.add).then_inc(S["dve"], 1)
            dve.wait_ge(S["dve"], b1)
            n_ov = dve.value_load(ovi[0:1, 15:16], min_val=0, max_val=OV)
            with dve.If(n_ov > 0):
                dve.wait_ge(S["ss2"], 6)
                v_.memset(wpick[:, :, CAP:P], 0.0)
                with dve.Fori(0, n_ov) as j:
                    build(CAP, j * 4 + (b1 + 1), j * 4 + (b1 + 2), "ov_p", j + 1)
                    build_weighted(CAP, j * 4 + (b1 + 3), j * 4 + (b1 + 4), "ov_wp", j + 1)
                    dve.wait_ge(S["ov_sel"], j + 1)
                    copy_xT(CAP).then_inc(S["ov_x"], 1)
                    dve.wait_ge(S["ov_u"], j + 1)
                    dve.wait_ge(S["ov_sil"], j + 1)
                    TT(hid[0:CAP, :].rearrange("p (k c) -> p k c", k=KE), in_order(ps[3], CAP), in_order(sil, CAP),
                       ALU.mult).then_inc(S["ov_hid"], 1)
                    for c in range(6):
                        dve.wait_ge(S["ov_sh"], j * 6 + SHARED[c])
                        add_share(c, "ov_add")
                    dve.wait_ge(S["ov_add"], j * 6 + 6)
                dve.sem_inc(S["fin_sum"], 1)
                dve.wait_ge(S["ov_ss"], 3)
            cnt[0], name[0] = 0, "dve_end"
            dve.wait_ge(S["ss2"], 6)
            rsqrt_rows(0, P, 3)
            for i, (t0, n) in enumerate(TOK):
                STT(h2[0:n, i, :], h2[0:n, i, :], rs[0:n, 1, i:i + 1], gfin[0:n, :], ALU.mult, ALU.mult).then_inc(
                    S["fin_done"], 1)


_INS = ["x_prompt", "x_sample", "state_hgrn", "state_s5_re", "state_s5_im", "norm_mix_g", "w_in", "hgrn_lb_raw",
        "hgrn_onorm_g", "w_branch_a", "s5_lambda_re", "s5_lambda_im", "s5_log_dt", "s5_b_re", "s5_b_im", "s5_c_re",
        "s5_c_im", "s5_d", "w_glu", "b_glu", "w_out", "norm_ffn_g", "w_router_group", "b_router_group",
        "w_router_expert", "b_router_expert", "w_exp_gate", "w_exp_up", "w_exp_down", "norm_final_g"]
_OUTS = [("y_p", (1, 256, 1024)), ("y_s", (8, 8, 1024)), ("hg_p", (1, 1, 8, 128, 128)), ("re_p", (1, 1, 32, 64)),
         ("im_p", (1, 1, 32, 64)), ("hg_s", (1, 8, 8, 128, 128)), ("re_s", (1, 8, 32, 64)), ("im_s", (1, 8, 32, 64))]


def kernel(**inputs):
    import numpy as _np
    import concourse.bacc as _bacc
    from concourse import mybir as _mybir
    from concourse.bass_utils import run_bass_kernel_spmd as _run

    nc = _bacc.Bacc("TRN2", target_bir_lowering=False, num_devices=1)
    arrays, ins, outs = {}, {}, {}
    for name in _INS:
        arr = _np.ascontiguousarray(inputs[name])
        arrays[f"in_{name}_dram"] = arr
        ins[name] = nc.dram_tensor(f"in_{name}_dram", arr.shape, _mybir.dt.from_np(arr.dtype), kind="ExternalInput").ap()
    for name, shape in _OUTS:
        outs[name] = nc.dram_tensor(f"out_{name}_dram", shape, _mybir.dt.float32, kind="ExternalOutput").ap()
    mixer_moe(nc, ins, outs)
    r = _run(nc, [arrays], core_ids=[0])
    return tuple(r.results[0][f"out_{name}_dram"] for name, _ in _OUTS)
```
